# Optimizing a Trainium2 kernel written in Bass

```python
import math
import jax
import jax.numpy as jnp
from jax import lax
import numpy as np

D_MODEL = 1024
BATCH = 1
SEQ = 256
DEPTH = 2

HEAD_DIM = 64
BRANCH_WIDTH = 256
N_BRANCH = 4
SB_HEADS = 4
Q_BLOCK = 128
S5_GROUPS = 16
S5_GROUP_CH = 16
S5_STATE = 64
S5_WIDTH = S5_GROUPS * S5_GROUP_CH
GLA_HEADS = 4
GLA_DK = 32
GLA_DV = 64
GLA_GATE_RANK = 16
GLA_GATE_NORM = 16.0
GLA_CHUNK = 64
DSA_HEADS = 4
DSA_PATTERNS = ((128, 1), (512, 4), (2048, 16))
DSA_BLOCK = 128
ROPE_THETA = 10000.0
D_FF = 2816
RMS_EPS = 1e-6
IN_SPLITS = (
    3 * SB_HEADS * HEAD_DIM,
    S5_WIDTH,
    GLA_HEADS * GLA_DK,
    GLA_HEADS * GLA_DK,
    GLA_HEADS * GLA_DV,
    GLA_HEADS * GLA_DV,
    GLA_GATE_RANK,
    3 * DSA_HEADS * HEAD_DIM,
    N_BRANCH * D_MODEL,
)
IN_WIDTH = sum(IN_SPLITS)

kernel_name = "hybrid_gated_four_mixer_macaron"

def rms_norm(x, g):
    x32 = x.astype(jnp.float32)
    y = x32 * lax.rsqrt(jnp.mean(x32 * x32, axis=-1, keepdims=True) + RMS_EPS)
    return (y * g.astype(jnp.float32)).astype(x.dtype)

def swiglu(x, w_in, w_out):
    a, b = jnp.split(x @ w_in, 2, axis=-1)
    return (jax.nn.silu(a) * b) @ w_out

def rope_tables(seq):
    inv = ROPE_THETA ** (-jnp.arange(0, HEAD_DIM, 2, dtype=jnp.float32) / HEAD_DIM)
    ang = jnp.arange(seq, dtype=jnp.float32)[:, None] * inv[None, :]
    return jnp.cos(ang), jnp.sin(ang)

def apply_rope(x, cos, sin):
    half = x.shape[-1] // 2
    x1, x2 = x[..., :half], x[..., half:]
    c, s = cos[None, :, None, :], sin[None, :, None, :]
    return jnp.concatenate([x1 * c - x2 * s, x2 * c + x1 * s], axis=-1)

def stick_breaking_attention(q, k, v):
    bsz, seq, heads, hd = q.shape
    nb = seq // Q_BLOCK
    qf = q.astype(jnp.float32) * (hd ** -0.5)
    kf = k.astype(jnp.float32)
    vf = v.astype(jnp.float32)
    q_blocks = qf.reshape(bsz, nb, Q_BLOCK, heads, hd).transpose(1, 0, 3, 2, 4)
    key_pos = jnp.arange(seq)

    def one_block(args):
        qb, blk = args
        z = jnp.einsum('bhqd,bshd->bhqs', qb, kf)
        q_pos = blk * Q_BLOCK + jnp.arange(Q_BLOCK)
        strict = key_pos[None, :] < q_pos[:, None]
        log_keep = jnp.where(strict, jax.nn.log_sigmoid(-z), 0.0)
        log_after = lax.cumsum(log_keep, axis=3, reverse=True) - log_keep
        w = jnp.where(strict, jnp.exp(jax.nn.log_sigmoid(z) + log_after), 0.0)
        return jnp.einsum('bhqs,bshd->bqhd', w, vf)

    out = lax.map(one_block, (q_blocks, jnp.arange(nb)))
    return out.transpose(1, 0, 2, 3, 4).reshape(bsz, seq, heads * hd)

def s5_mixer(u, lam_re, lam_im, log_step, b_re, b_im, c_re, c_im, d_skip, w_glu):
    bsz, seq, _ = u.shape
    uf = u.astype(jnp.float32).reshape(bsz, seq, S5_GROUPS, S5_GROUP_CH)
    lam = lax.complex(lam_re.astype(jnp.float32), lam_im.astype(jnp.float32))
    dt = jnp.exp(log_step.astype(jnp.float32))[:, None]
    lam_bar = jnp.exp(lam * dt)
    b_mat = lax.complex(b_re.astype(jnp.float32), b_im.astype(jnp.float32))
    b_bar = ((lam_bar - 1.0) / lam)[..., None] * b_mat
    c_mat = lax.complex(c_re.astype(jnp.float32), c_im.astype(jnp.float32))
    bu = jnp.einsum('bsgh,gph->bsgp', uf.astype(jnp.complex64), b_bar)
    a = jnp.broadcast_to(lam_bar, bu.shape)

    def combine(e1, e2):
        a1, b1 = e1
        a2, b2 = e2
        return a1 * a2, a2 * b1 + b2

    _, states = lax.associative_scan(combine, (a, bu), axis=1)
    y = jnp.einsum('bsgp,ghp->bsgh', states, c_mat).real + d_skip.astype(jnp.float32) * uf
    y = jax.nn.gelu(y.reshape(bsz, seq, S5_WIDTH))
    ga, gb = jnp.split(y @ w_glu.astype(jnp.float32), 2, axis=-1)
    return ga * jax.nn.sigmoid(gb)

def gla_mixer(q, k, v, r, g1, w_gate, b_gate, norm_g):
    bsz, seq, _ = q.shape
    nc = seq // GLA_CHUNK
    z = g1.astype(jnp.float32) @ w_gate.astype(jnp.float32) + b_gate.astype(jnp.float32)
    log_a = jax.nn.log_sigmoid(z) / GLA_GATE_NORM

    def heads(t, dh):
        t = t.astype(jnp.float32).reshape(bsz, nc, GLA_CHUNK, GLA_HEADS, dh)
        return t.transpose(1, 0, 3, 2, 4)

    qc = heads(q, GLA_DK) * (GLA_DK ** -0.5)
    kc = heads(k, GLA_DK)
    vc = heads(v, GLA_DV)
    gc = heads(log_a, GLA_DK)
    causal = jnp.tril(jnp.ones((GLA_CHUNK, GLA_CHUNK), dtype=bool))

    def step(state, inp):
        qi, ki, vi, gi = inp
        bcum = jnp.cumsum(gi, axis=2)
        o_inter = jnp.einsum('bhcd,bhde->bhce', qi * jnp.exp(bcum), state)
        diff = bcum[:, :, :, None, :] - bcum[:, :, None, :, :]
        decay = jnp.exp(jnp.where(causal[:, :, None], diff, -jnp.inf))
        att = jnp.einsum('bhid,bhjd,bhijd->bhij', qi, ki, decay)
        o = o_inter + jnp.einsum('bhij,bhje->bhie', att, vi)
        blast = bcum[:, :, -1:, :]
        state = jnp.exp(blast[:, :, 0, :])[..., None] * state + jnp.einsum(
            'bhcd,bhce->bhde', ki * jnp.exp(blast - bcum), vi)
        return state, o

    s0 = jnp.zeros((bsz, GLA_HEADS, GLA_DK, GLA_DV), jnp.float32)
    _, o = lax.scan(step, s0, (qc, kc, vc, gc))
    o = o.transpose(1, 0, 3, 2, 4).reshape(bsz, seq, GLA_HEADS, GLA_DV)
    o = rms_norm(o, norm_g.reshape(GLA_HEADS, GLA_DV))
    return o.reshape(bsz, seq, GLA_HEADS * GLA_DV) * jax.nn.silu(r.astype(jnp.float32))

def to_residue(t, dil, padded):
    bsz, seq, heads, hd = t.shape
    t = jnp.pad(t, ((0, 0), (0, padded - seq), (0, 0), (0, 0)))
    t = t.reshape(bsz, padded // dil, dil, heads, hd).transpose(0, 2, 3, 1, 4)
    return t.reshape(bsz * dil * heads, padded // dil, hd)

def from_residue(t, bsz, dil, heads, seq):
    rest = t.shape[2:]
    length = t.shape[1]
    t = jnp.moveaxis(t.reshape((bsz, dil, heads, length) + rest), 3, 1)
    return t.reshape((bsz, length * dil, heads) + rest)[:, :seq]

def banded_window_attention(q, k, v, n_steps):
    rows, length, hd = q.shape
    nb = length // DSA_BLOCK
    qb = q.reshape(rows, nb, DSA_BLOCK, hd)

    def key_blocks(t):
        tp = jnp.pad(t, ((0, 0), (DSA_BLOCK, 0), (0, 0)))
        prev = tp[:, :length].reshape(rows, nb, DSA_BLOCK, hd)
        cur = tp[:, DSA_BLOCK:].reshape(rows, nb, DSA_BLOCK, hd)
        return jnp.concatenate([prev, cur], axis=2)

    kb, vb = key_blocks(k), key_blocks(v)
    s = jnp.einsum('nbqd,nbkd->nbqk', qb, kb) * (hd ** -0.5)
    qi = jnp.arange(DSA_BLOCK)[:, None]
    kj = jnp.arange(2 * DSA_BLOCK)[None, :]
    dist = qi + DSA_BLOCK - kj
    key_idx = jnp.arange(nb)[:, None, None] * DSA_BLOCK + kj[None] - DSA_BLOCK
    valid = ((dist >= 0) & (dist <= n_steps))[None] & (key_idx >= 0)
    s = jnp.where(valid, s, -jnp.inf)
    lse = jax.nn.logsumexp(s, axis=-1)
    p = jnp.exp(s - lse[..., None])
    o = jnp.einsum('nbqk,nbkd->nbqd', p, vb)
    return o.reshape(rows, length, hd), lse.reshape(rows, length)

def dilated_mixer(q, k, v, q_norm, k_norm, cos, sin):
    bsz, seq, heads, hd = q.shape
    qf = apply_rope(rms_norm(q.astype(jnp.float32), q_norm), cos, sin)
    kf = apply_rope(rms_norm(k.astype(jnp.float32), k_norm), cos, sin)
    vf = v.astype(jnp.float32)
    outs, lses = [], []
    for window, dil in DSA_PATTERNS:
        span = dil * DSA_BLOCK
        padded = -(-seq // span) * span
        o, lse = banded_window_attention(to_residue(qf, dil, padded), to_residue(kf, dil, padded),
                                         to_residue(vf, dil, padded), window // dil)
        outs.append(from_residue(o, bsz, dil, heads, seq))
        lses.append(from_residue(lse, bsz, dil, heads, seq))
    w = jax.nn.softmax(jnp.stack(lses, axis=0), axis=0)
    out = jnp.sum(w[..., None] * jnp.stack(outs, axis=0), axis=0)
    return out.reshape(bsz, seq, heads * hd)

def hybrid_layer(x, cos, sin, ffn1_norm, ffn1_w_in, ffn1_w_out, mix_norm, w_in,
                 s5_lam_re, s5_lam_im, s5_log_step, s5_b_re, s5_b_im, s5_c_re, s5_c_im, s5_d, s5_w_glu,
                 gla_w_gate, gla_b_gate, gla_norm, dsa_q_norm, dsa_k_norm, w_branch, w_out,
                 ffn2_norm, ffn2_w_in, ffn2_w_out):
    bsz, seq, _ = x.shape
    h = x + 0.5 * swiglu(rms_norm(x, ffn1_norm), ffn1_w_in, ffn1_w_out)
    u = rms_norm(h, mix_norm)
    proj = u @ w_in
    (sb_qkv, s5_u, gq, gk, gv, gr, gg, dsa_qkv, gates) = jnp.split(
        proj, np.cumsum(IN_SPLITS)[:-1].tolist(), axis=-1)

    sb_q, sb_k, sb_v = [t.reshape(bsz, seq, SB_HEADS, HEAD_DIM) for t in jnp.split(sb_qkv, 3, axis=-1)]
    y_sb = stick_breaking_attention(sb_q, sb_k, sb_v)
    y_s5 = s5_mixer(s5_u, s5_lam_re, s5_lam_im, s5_log_step, s5_b_re, s5_b_im, s5_c_re, s5_c_im,
                    s5_d, s5_w_glu)
    y_gla = gla_mixer(gq, gk, gv, gr, gg, gla_w_gate, gla_b_gate, gla_norm)
    d_q, d_k, d_v = [t.reshape(bsz, seq, DSA_HEADS, HEAD_DIM) for t in jnp.split(dsa_qkv, 3, axis=-1)]
    y_dsa = dilated_mixer(d_q, d_k, d_v, dsa_q_norm, dsa_k_norm, cos, sin)

    branches = jnp.stack([y_sb, y_s5, y_gla, y_dsa], axis=2).astype(x.dtype)
    gate = jax.nn.sigmoid(gates.reshape(bsz, seq, N_BRANCH, D_MODEL))
    per_branch = jnp.einsum('bsnw,nwd->bsnd', branches, w_branch)
    mixed = jnp.sum(gate * per_branch, axis=2)
    h = h + mixed @ w_out
    return h + 0.5 * swiglu(rms_norm(h, ffn2_norm), ffn2_w_in, ffn2_w_out)

def setup_inputs(seed: int = 0) -> dict:
    key = jax.random.key(seed)
    ks = jax.random.split(key, 26)
    f32 = jnp.float32
    L = DEPTH
    G, P, H = S5_GROUPS, S5_STATE, S5_GROUP_CH

    def normal(k, shape, scale):
        return jax.random.normal(k, shape, f32) * scale

    def gain(k, n):
        return 1.0 + 0.02 * jax.random.normal(k, (L, n), f32)

    return {
        'x': normal(ks[0], (BATCH, SEQ, D_MODEL), 1.0),
        'ffn1_norm': gain(ks[1], D_MODEL),
        'ffn1_w_in': normal(ks[2], (L, D_MODEL, 2 * D_FF), D_MODEL ** -0.5),
        'ffn1_w_out': normal(ks[3], (L, D_FF, D_MODEL), D_FF ** -0.5),
        'mix_norm': gain(ks[4], D_MODEL),
        'w_in': normal(ks[5], (L, D_MODEL, IN_WIDTH), D_MODEL ** -0.5),
        's5_lam_re': -0.5 + normal(ks[6], (L, G, P), 0.01),
        's5_lam_im': jnp.pi * jnp.arange(P, dtype=f32) + normal(ks[7], (L, G, P), 0.01),
        's5_log_step': jax.random.uniform(ks[8], (L, G), f32, math.log(1e-3), math.log(1e-1)),
        's5_b_re': normal(ks[9], (L, G, P, H), (2 * H) ** -0.5),
        's5_b_im': normal(ks[10], (L, G, P, H), (2 * H) ** -0.5),
        's5_c_re': normal(ks[11], (L, G, H, P), P ** -0.5),
        's5_c_im': normal(ks[12], (L, G, H, P), P ** -0.5),
        's5_d': normal(ks[13], (L, G, H), 1.0),
        's5_w_glu': normal(ks[14], (L, S5_WIDTH, 2 * S5_WIDTH), S5_WIDTH ** -0.5),
        'gla_w_gate': normal(ks[15], (L, GLA_GATE_RANK, GLA_HEADS * GLA_DK), GLA_GATE_RANK ** -0.5),
        'gla_b_gate': normal(ks[16], (L, GLA_HEADS * GLA_DK), 0.01),
        'gla_norm': gain(ks[17], GLA_HEADS * GLA_DV),
        'dsa_q_norm': gain(ks[18], HEAD_DIM),
        'dsa_k_norm': gain(ks[19], HEAD_DIM),
        'w_branch': normal(ks[20], (L, N_BRANCH, BRANCH_WIDTH, D_MODEL), BRANCH_WIDTH ** -0.5),
        'w_out': normal(ks[21], (L, D_MODEL, D_MODEL), D_MODEL ** -0.5),
        'ffn2_norm': gain(ks[22], D_MODEL),
        'ffn2_w_in': normal(ks[23], (L, D_MODEL, 2 * D_FF), D_MODEL ** -0.5),
        'ffn2_w_out': normal(ks[24], (L, D_FF, D_MODEL), D_FF ** -0.5),
    }

def reference(x, ffn1_norm, ffn1_w_in, ffn1_w_out, mix_norm, w_in, s5_lam_re, s5_lam_im, s5_log_step,
              s5_b_re, s5_b_im, s5_c_re, s5_c_im, s5_d, s5_w_glu, gla_w_gate, gla_b_gate, gla_norm,
              dsa_q_norm, dsa_k_norm, w_branch, w_out, ffn2_norm, ffn2_w_in, ffn2_w_out):
    cos, sin = rope_tables(x.shape[1])
    h = x
    for l in range(DEPTH):
        h = hybrid_layer(h, cos, sin, ffn1_norm[l], ffn1_w_in[l], ffn1_w_out[l], mix_norm[l], w_in[l],
                         s5_lam_re[l], s5_lam_im[l], s5_log_step[l], s5_b_re[l], s5_b_im[l],
                         s5_c_re[l], s5_c_im[l], s5_d[l], s5_w_glu[l], gla_w_gate[l], gla_b_gate[l],
                         gla_norm[l], dsa_q_norm[l], dsa_k_norm[l], w_branch[l], w_out[l],
                         ffn2_norm[l], ffn2_w_in[l], ffn2_w_out[l])
    return h


_drawn_inputs = setup_inputs


def setup_inputs(seed=0):
    import zlib

    import numpy as np

    out = dict(_drawn_inputs(seed))
    spreads = {}
    factors = {'ffn1_norm': 3.911,
     's5_lam_re': 64.0,
     's5_lam_im': 25.8,
     's5_log_step': 25.704,
     's5_b_re': 36.04,
     's5_b_im': 37.248,
     's5_c_re': 36.208,
     's5_c_im': 36.904,
     'gla_b_gate': 8.0,
     'gla_norm': 28.752,
     'dsa_q_norm': 22.912,
     'dsa_k_norm': 23.674,
     'ffn2_norm': 5.43}
    for name, (base, spread) in spreads.items():
        noise = np.random.default_rng([zlib.crc32(name.encode()), seed]).standard_normal(out[name].shape)
        drawn = base * np.exp(spread * noise) if base else spread * noise
        out[name] = jnp.asarray(drawn.astype(out[name].dtype))
    for name, factor in factors.items():
        out[name] = (out[name] * factor).astype(out[name].dtype)
    return out
```

```python
import math
from contextlib import ExitStack

import numpy as np

import concourse.bass as bass
from concourse import mybir

F32 = mybir.dt.float32
F32R = mybir.dt.float32r
ACT = mybir.ActivationFunctionType
ALU = mybir.AluOpType
AX = mybir.AxisListType

P = 128
LAYERS = 2
T = 256
D = 1024
KT = D // P
DFF = 2816
FT = DFF // P
BW = 256
HEADS = 4
EPS = 1e-6

BLK = 2048
HALF = BLK // 2
RING = 3
FFN_BLOCKS = FT + FT // 2
PROJ = ["s5u", "sbq", "sbk", "gg", "dq", "dk", "gqk", "sbv", "dv", "gv", "gr"]
NPROJ = len(PROJ)
NGATE = 16
NBRANCH = 4
OUT_TILES = [(0, 1), (2, 3), (4, 5), (6,), (7,)]
MIX_BLOCKS = NPROJ + NGATE + NBRANCH + len(OUT_TILES)
PER_LAYER = 2 * FFN_BLOCKS + MIX_BLOCKS
assert PER_LAYER % RING == 0 and FFN_BLOCKS % RING == 0 and MIX_BLOCKS % RING == 0
NATURAL = {"dq", "dk", "sbv", "dv", "gv"}
SLOT = {name: m for m, name in enumerate(PROJ)}

ATT = T + P

GC = 32
NGC = T // GC
GLA_CLIP = 85.0 * 16

STATES = 1024
ST = STATES // P

CONST = {}
_at = 0
for _name, _n in [("ident", P), ("head_ones", P), ("neg_suffix", P), ("neg_ones", P),
                  ("causal", ATT), ("strict", ATT), ("count", ATT), ("forbid", ATT),
                  ("cos", 2 * 64), ("sin", 2 * 64), ("scalars", 6)]:
    CONST[_name] = (_at, _n)
    _at += _n
NCONST = _at

PARAM = {}
_at = 0
for _name, _n in [("g_ffn1", KT), ("g_mix", KT), ("g_ffn2", KT), ("gla_norm", 2), ("b_gate", 1),
                  ("s5_d", 2), ("lam_re", ST), ("lam_im", ST), ("log_step", ST),
                  ("dsa_gain", 2 * 64), ("w_gate", P), ("s5_b", 2 * 2 * P), ("s5_c", 2 * ST * 32),
                  ("w_glu", 2 * 2 * BW)]:
    PARAM[_name] = (_at, _n)
    _at += _n
NPARAM = _at

class PER:
    w_hi = 2 * PER_LAYER
    w_lo = 2 * PER_LAYER
    w_used = PER_LAYER
    h_silu = 2 * FT
    h_prod = 2 * FT
    h_hi = 2 * FT
    h_lo = 2 * FT
    ffn_acc = 6
    res = 12
    sq = 12
    ss = 3
    v = 3
    y0 = 3
    u = 24
    u_hi = 24
    u_lo = 24
    evac = NPROJ + NGATE
    s5_exp = 1
    s5_red = 1
    s5_trig = 1
    s5_tab = 1
    s5_r = 1
    s5_rden = 1
    s5_coef = 1
    s5_p = ST
    s5_rot = ST
    s5_x = ST
    s5_scan = ST
    s5_state = ST
    s5_y = ST
    s5_inner = 1
    s5_tanh = 1
    s5_gelu = 1
    s5_glu = 1
    s5_sig = 1
    sb_z = HEADS
    sb_ln = HEADS
    sb_sp = HEADS
    sb_acc = HEADS
    sb_exp = HEADS
    sb_w = HEADS
    sb_o = 1
    gla_z = 1
    gla_ln = 1
    gla_arg = 1
    gla_exp = 1
    gla_kq = 1
    gla_att = HEADS
    gla_attm = HEADS
    gla_o = 1
    gla_oc = 1
    gla_sq = 1
    gla_ss = 1
    gla_v = 1
    gla_y0 = 1
    gla_tanh = 1
    dsa_sq = 1
    dsa_ms = 1
    dsa_y0 = 1
    dsa_rope = 1
    dsa_t = 1
    dsa_qk = 2
    dsa_s = HEADS
    dsa_max = HEADS
    dsa_exp = HEADS
    dsa_p = HEADS
    dsa_pt = HEADS
    dsa_pte = HEADS
    dsa_o = 1
    y = 4
    b_hi = 4
    b_lo = 4
    pb_half = 4
    gated = 8
    mixed = 8
    m_hi = 8
    m_lo = 8
    dve = 62
    act = 16
    pool = 216


class Signals:
    pass


TWO_PI = 2 * math.pi
PI_A = 6.28125
PI_B = float(np.float32(TWO_PI - PI_A))
PI_C = float(TWO_PI - PI_A - PI_B)
ROUND = 1.5 * 2.0 ** 23
PI_BELOW = 3.14159250259


class Steps:

    def __init__(self, eng, sem, layer, per):
        self.eng, self.sem, self.layer, self.per, self.n = eng, sem, layer, per, 0

    def mark(self, ins):
        ins.then_inc(self.sem, 1)
        self.n += 1
        return self.n

    def wait(self, n):
        self.eng.wait_ge(self.sem, self.layer * self.per + n)

    def link(self, ins):
        self.wait(self.mark(ins))


def build(nc, x_in, stream, params_in, const_in, out):
    ctx = ExitStack()
    with ctx:
        def sb(name, shape, dt=F32):
            return ctx.enter_context(nc.sbuf_tensor(name, shape, dt))

        def sem(name):
            return ctx.enter_context(nc.semaphore(name))

        raw = sb("raw", [P, RING, BLK])
        w_hi = sb("w_hi_t", [P, RING, BLK], F32R)
        w_lo = sb("w_lo_t", [P, RING, BLK], F32R)
        hT = sb("hT", [P, KT, T])
        U = sb("U", [P, KT, T])
        u_hi = sb("u_hi_t", [P, KT, T], F32R)
        u_lo = sb("u_lo_t", [P, KT, T], F32R)
        G = sb("G", [P, 4, KT, T])
        b_hi = sb("b_hi_t", [P, 4, 2, T], F32R)
        b_lo = sb("b_lo_t", [P, 4, 2, T], F32R)
        h_hi = sb("h_hi_t", [P, 2, T], F32R)
        h_lo = sb("h_lo_t", [P, 2, T], F32R)
        cst = sb("cst", [P, NCONST])
        prm = sb("prm", [P, NPARAM])
        yb = sb("yb", [P, 2, 2, T])
        attA = sb("attA", [P, HEADS, ATT])
        attB = sb("attB", [P, HEADS, ATT])
        s5u = sb("s5u", [P, 2, T])
        s5x = sb("s5x", [P, 2, 2, 2, T])
        st = sb("st", [P, 2, 2, T])
        s5n = sb("s5n", [P, 25, ST])
        s5c = sb("s5c", [P, 2, ST, 32])
        sbqk = sb("sbqk", [P, 2, 2, T])
        sbv = sb("sbv", [P, 2, T])
        gqk = sb("gqk", [P, 2, T])
        gq = sb("gq", [P, T])
        dqk = sb("dqk", [P, 2, 8, 64])
        dv = sb("dv", [P, 2, T])
        dms = sb("dms", [P, 5, 16])
        dmx = sb("dmx", [P, HEADS, 6])

        rotC, rotS = G[:, 2, :, :], G[:, 3, :, :]
        nrm = yb[:, :, :, :].rearrange("p a b t -> p (a b) t")
        a_s, hf = sbqk[:, 0, :, :], sbqk[:, 1, :, :]
        sbq, sbk = sbqk[:, 0, :, :], sbqk[:, 1, :, :]
        gv, gr = sbqk[:, 0, :, :], sbqk[:, 1, :, :]
        sbt = attB[:, 0:2, :]
        gB = attB[:, 2:4, :].rearrange("p h c -> p (h c)").rearrange("p (k t) -> p k t", k=3)
        kd = U[:, 0:6, :].rearrange("p a t -> p (a t)")
        gn = U[:, :, :].rearrange("p (k a) t -> p k (a t)", k=4)
        ropeX = attB[:, :, :].rearrange("p h c -> p (h c)")[:, 0:2 * 8 * 64] \
            .rearrange("p (t h d) -> p t h d", t=2, h=8)
        dqT = dqk[:, 0, :, :].rearrange("p h d -> p (h d)")
        dkT = dqk[:, 1, :, :].rearrange("p h d -> p (h d)")
        s5g = s5x[:, :, :, :, :].rearrange("p a b c t -> p (a b) (c t)")
        prods = [attA[:, :, 0:T], attB[:, :, 0:T]]
        tabA = attA[:, :, :].rearrange("p h c -> p (h c)")
        tabB = attB[:, :, :].rearrange("p h c -> p (h c)")

        banks = ctx.enter_context(nc.psum_tensor("banks", [P, 8, 512], F32))

        landed = [sem(f"landed{i}") for i in range(RING)]
        s = Signals()
        s.w_hi = sem("w_hi")
        s.w_lo = sem("w_lo")
        s.w_used = sem("w_used")
        s.h_silu = sem("h_silu")
        s.h_prod = sem("h_prod")
        s.h_hi = sem("h_hi")
        s.h_lo = sem("h_lo")
        s.ffn_acc = sem("ffn_acc")
        s.res = sem("res")
        s.sq = sem("sq")
        s.ss = sem("ss")
        s.v = sem("v")
        s.y0 = sem("y0")
        s.u = sem("u")
        s.u_hi = sem("u_hi")
        s.u_lo = sem("u_lo")
        s.evac = sem("evac")
        s.s5_exp = sem("s5_exp")
        s.s5_red = sem("s5_red")
        s.s5_trig = sem("s5_trig")
        s.s5_tab = sem("s5_tab")
        s.s5_r = sem("s5_r")
        s.s5_rden = sem("s5_rden")
        s.s5_coef = sem("s5_coef")
        s.s5_p = sem("s5_p")
        s.s5_rot = sem("s5_rot")
        s.s5_x = sem("s5_x")
        s.s5_scan = sem("s5_scan")
        s.s5_state = sem("s5_state")
        s.s5_y = sem("s5_y")
        s.s5_inner = sem("s5_inner")
        s.s5_tanh = sem("s5_tanh")
        s.s5_gelu = sem("s5_gelu")
        s.s5_glu = sem("s5_glu")
        s.s5_sig = sem("s5_sig")
        s.sb_z = sem("sb_z")
        s.sb_ln = sem("sb_ln")
        s.sb_sp = sem("sb_sp")
        s.sb_acc = sem("sb_acc")
        s.sb_exp = sem("sb_exp")
        s.sb_w = sem("sb_w")
        s.sb_o = sem("sb_o")
        s.gla_z = sem("gla_z")
        s.gla_ln = sem("gla_ln")
        s.gla_arg = sem("gla_arg")
        s.gla_exp = sem("gla_exp")
        s.gla_kq = sem("gla_kq")
        s.gla_att = sem("gla_att")
        s.gla_attm = sem("gla_attm")
        s.gla_o = sem("gla_o")
        s.gla_oc = sem("gla_oc")
        s.gla_sq = sem("gla_sq")
        s.gla_ss = sem("gla_ss")
        s.gla_v = sem("gla_v")
        s.gla_y0 = sem("gla_y0")
        s.gla_tanh = sem("gla_tanh")
        s.dsa_sq = sem("dsa_sq")
        s.dsa_ms = sem("dsa_ms")
        s.dsa_y0 = sem("dsa_y0")
        s.dsa_rope = sem("dsa_rope")
        s.dsa_t = sem("dsa_t")
        s.dsa_qk = sem("dsa_qk")
        s.dsa_s = sem("dsa_s")
        s.dsa_max = sem("dsa_max")
        s.dsa_exp = sem("dsa_exp")
        s.dsa_p = sem("dsa_p")
        s.dsa_pt = sem("dsa_pt")
        s.dsa_pte = sem("dsa_pte")
        s.dsa_o = sem("dsa_o")
        s.y = sem("y")
        s.b_hi = sem("b_hi")
        s.b_lo = sem("b_lo")
        s.pb_half = sem("pb_half")
        s.gated = sem("gated")
        s.mixed = sem("mixed")
        s.m_hi = sem("m_hi")
        s.m_lo = sem("m_lo")
        s.dve = sem("dve")
        s.act = sem("act")
        s.pool = sem("pool")
        s_x = sem("x_landed")
        s_const = sem("const_landed")
        s_params = sem("params_landed")
        s_out = sem("out_stored")

        def c(name, rows=P):
            a, n = CONST[name]
            return cst[0:rows, a:a + n]

        def p_(name):
            a, n = PARAM[name]
            return prm[:, a:a + n]

        eps_c, half_pi_c, one_c = (c("scalars")[:, i:i + 1] for i in range(3))

        block = ctx.enter_context(nc.Block())

        @block.sync
        def _(sp):
            def load(n, slot):
                sp.dma_start(raw[:, slot, :], stream[n]).then_inc(landed[slot], 16)

            sp.dma_start(hT[:, :, :], x_in).then_inc(s_x, 16)
            sp.dma_start(cst[:, :], const_in).then_inc(s_const, 16)
            sp.dma_start(prm[:, :], params_in[0]).then_inc(s_params, 16)
            for slot in range(RING):
                load(slot, slot)
            with sp.Fori(0, LAYERS) as layer:
                def next_three(n0):
                    for slot in range(RING):
                        sp.wait_ge(s.w_lo, layer * PER.w_lo + 2 * n0 + 2 * slot + 2)
                        load(layer * PER_LAYER + n0 + slot, slot)

                with sp.Fori(0, PER_LAYER // RING - 1) as t:
                    next_three(t * RING + RING)
                sp.wait_ge(s.u, layer * PER.u + 24)
                sp.dma_start(prm[:, :], params_in[layer + 1]).then_inc(s_params, 16)
                next_three(PER_LAYER)
            for q in range(4):
                sp.wait_ge(s.res, 4 + (LAYERS - 1) * PER.res + 8 + q + 1)
                sp.dma_start(out[:, 2 * q:2 * q + 2, :], hT[:, 2 * q:2 * q + 2, :]).then_inc(s_out, 16)
            sp.wait_ge(s_out, 4 * 16)
            sp.wait_ge(s_params, (LAYERS + 1) * 16)

        @block.tensor
        def _(pe):
            pe.sem_inc(s.w_used, RING)
            pe.wait_ge(s_const, 16)

            def three(o, st, mv, start, stop, inc=None):
                pe.matmul(o, st[0], mv[0], start=start, stop=False, skip_group_check=True)
                pe.matmul(o, st[0], mv[1], start=False, stop=False, skip_group_check=True)
                ins = pe.matmul(o, st[1], mv[0], start=False, stop=stop, skip_group_check=True)
                if inc is not None:
                    ins.then_inc(inc, 1)

            def w(slot, a, n):
                return w_hi[:, slot, a:a + n], w_lo[:, slot, a:a + n]

            def act_tiles(kt, a=0, n=T):
                return u_hi[:, kt, a:a + n], u_lo[:, kt, a:a + n]

            def single(o, st, mv, start=True, stop=True):
                return pe.matmul(o, st, mv, start=start, stop=stop, skip_group_check=True)

            with pe.Fori(0, LAYERS) as layer:
                def block_ready(b):
                    pe.wait_ge(s.w_lo, layer * PER.w_lo + 2 * b + 8)

                def in_block(b, slot, bank, norm=None):
                    block_ready(b)
                    for kt in range(KT):
                        if norm is not None:
                            pe.wait_ge(s.u_lo, layer * PER.u_lo + 8 * norm + kt + 1)
                        for ct in range(2):
                            last = kt == KT - 1 and ct == 1
                            three(banks[:, bank, ct * T:(ct + 1) * T], w(slot, kt * 256 + ct * P, P),
                                  act_tiles(kt), kt == 0 and ct == 0, last, s.w_used if last else None)

                def natural_block(b, slot, bank):
                    block_ready(b)
                    for kt in range(KT):
                        for tt in range(2):
                            last = kt == KT - 1 and tt == 1
                            three(banks[:, bank, tt * BW:(tt + 1) * BW], act_tiles(kt, tt * P, P),
                                  w(slot, kt * 256, 256), kt == 0 and tt == 0, last,
                                  s.w_used if last else None)

                def sum_squares(norm, bank):
                    for kt in range(KT):
                        if kt % 2 == 0:
                            pe.wait_ge(s.sq, layer * PER.sq + 4 * norm + kt // 2 + 1)
                        ins = single(banks[:, bank, 0:T], c("neg_ones"), U[:, kt, :], kt == 0, kt == KT - 1)
                    ins.then_inc(s.ss, 1)

                def ffn(f, b0):
                    def out_block(i, b, slot, tiles_first):
                        block_ready(b)
                        pe.wait_ge(s.h_lo, layer * PER.h_lo + FT * f + 2 * i + 2)
                        order = [(dt, k) for dt in range(KT) for k in range(2)] if tiles_first else \
                                [(dt, k) for k in range(2) for dt in range(KT)]
                        for dt, k in order:
                            first = isinstance(i, int) and i == 0 and k == 0
                            o = banks[:, dt // 2, (dt % 2) * T:(dt % 2 + 1) * T]
                            last = (dt, k) == order[-1]
                            three(o, w(slot, k * D + dt * P, P), (h_hi[:, k, :], h_lo[:, k, :]),
                                  first and dt % 2 == 0, False, s.w_used if last else
                                  (s.ffn_acc if tiles_first and k == 1 and dt % 2 == 1 else None))

                    in_block(b0, b0 % 3, 4, norm=0 if f == 0 else 2)
                    in_block(b0 + 1, (b0 + 1) % 3, 5)

                    def body(i, first):
                        pe.wait_ge(s.h_prod, layer * PER.h_prod + FT * f + 2 * i - 1)
                        in_block(b0 + 3 * i - 1, (b0 + 2) % 3, 4)
                        out_block(0 if first else i - 1, b0 + 3 * i, b0 % 3, False)
                        pe.wait_ge(s.h_prod, layer * PER.h_prod + FT * f + 2 * i)
                        in_block(b0 + 3 * i + 1, (b0 + 1) % 3, 5)

                    body(1, True)
                    with pe.Fori(2, FT // 2) as i:
                        body(i, False)
                    out_block(FT // 2 - 1, b0 + FFN_BLOCKS - 1, (b0 + 2) % 3, True)

                def mixer():
                    b0 = FFN_BLOCKS
                    head = lambda t, h, a, n: t[64 * (h % 2):64 * (h % 2) + 64, h // 2, a:a + n]

                    def scores(o_bank, k, q, h):
                        single(banks[:, o_bank, 0:T], head(k, h, 0, P), head(q, h, 0, T))
                        return single(banks[:, o_bank, T:ATT], head(k, h, P, P), head(q, h, P, P), start=False)

                    def attend(bank, v, att):
                        for h in range(HEADS):
                            o = banks[64 * (h % 2):64 * (h % 2) + 64, bank, (h // 2) * T:(h // 2 + 1) * T]
                            single(o, v[:, 0, 64 * h:64 * h + 64], att[:, h, 0:T], h < 2, False)
                            ins = single(o[:, P:T], v[:, 1, 64 * h:64 * h + 64], att[:, h, T:ATT], False, True)
                        return ins

                    def s5_in(i):
                        if i == 0:
                            pe.wait_ge(s.evac, layer * PER.evac + SLOT["s5u"] + 1)
                        if i >= 2:
                            pe.wait_ge(s.s5_rot, layer * PER.s5_rot + i - 1)
                        q = 32 * (i % 4)
                        for part in range(2):
                            a = PARAM["s5_b"][0] + (part * 2 + i // 4) * P
                            ins = single(banks[:, 6 + i % 2, part * T:(part + 1) * T], prm[q:q + 32, a:a + P],
                                         s5u[q:q + 32, i // 4, :], part == 0, True)
                        ins.then_inc(s.s5_p, 1)

                    def s5_out(i):
                        pe.wait_ge(s.s5_state, layer * PER.s5_state + i + 1)
                        if i == 0:
                            pe.wait_ge(s.s5_coef, layer * PER.s5_coef + 1)
                        q = 32 * (i % 4)
                        o = banks[q:q + 32, 3, (i // 4) * T:(i // 4 + 1) * T]
                        single(o, s5c[:, 0, i, :], st[:, i % 2, 0, :], i < 4, False)
                        single(o, s5c[:, 1, i, :], st[:, i % 2, 1, :], False, True).then_inc(s.s5_y, 1)

                    def sb_scores(h):
                        pe.wait_ge(s.evac, layer * PER.evac + SLOT["sbk"] + 1)
                        if h >= 2:
                            pe.wait_ge(s.sb_exp, layer * PER.sb_exp + h - 1)
                        scores(4 + h % 2, sbk, sbq, h).then_inc(s.sb_z, 1)

                    def sb_suffix(h):
                        pe.wait_ge(s.sb_sp, layer * PER.sb_sp + h + 1)
                        bank = 4 + h % 2
                        single(banks[:, bank, 0:T], c("neg_suffix"), attA[:, h, 0:T], False, False)
                        single(banks[:, bank, P:T], c("neg_ones"), attA[:, h, T:ATT], False, False)
                        single(banks[:, bank, T:ATT], c("neg_suffix"), attA[:, h, T:ATT], False, True) \
                            .then_inc(s.sb_acc, 1)

                    def gla_scores(h):
                        pe.wait_ge(s.gla_kq, layer * PER.gla_kq + 1)
                        pe.wait_ge(s.sb_exp, layer * PER.sb_exp + HEADS)
                        if h >= 2:
                            pe.wait_ge(s.gla_attm, layer * PER.gla_attm + h - 1)
                        r = slice(32 * h, 32 * h + 32)
                        first = True
                        for i in range(NGC):
                            at = P * i if i < 4 else P * 4 + T * (i - 4)
                            for jt in range(1 if i < 4 else 2):
                                col = GC * i if jt == 0 else T + GC * i - P
                                ins = single(banks[:, 4 + h % 2, col:col + GC], kd[r, at + jt * P:at + (jt + 1) * P],
                                             gq[r, GC * i:GC * i + GC], first, True)
                                first = False
                        ins.then_inc(s.gla_att, 1)

                    def dsa_scores(h):
                        pe.wait_ge(s.dsa_qk, layer * PER.dsa_qk + 2)
                        if h >= 2:
                            pe.wait_ge(s.dsa_max, layer * PER.dsa_max + h - 1)
                        hd = lambda t, a, n: t[64 * (h % 2):64 * (h % 2) + 64, (h // 2) * T + a:(h // 2) * T + a + n]
                        single(banks[:, 6 + h % 2, 0:P], hd(dqT, 0, P), hd(dkT, 0, P))
                        single(banks[:, 6 + h % 2, P:ATT], hd(dqT, P, P), hd(dkT, 0, T), False) \
                            .then_inc(s.dsa_s, 1)

                    def dsa_turn(h):
                        pe.wait_ge(s.dsa_p, layer * PER.dsa_p + h + 1)
                        if h < 2:
                            pe.wait_ge(s.dsa_max, layer * PER.dsa_max + h + 3)
                        else:
                            pe.wait_ge(s.dsa_pte, layer * PER.dsa_pte + h - 1)
                        for j in range(3):
                            ins = pe.transpose(banks[:, 6 + h % 2, j * P:(j + 1) * P], attB[:, h, j * P:(j + 1) * P],
                                               c("ident"))
                        ins.then_inc(s.dsa_pt, 1)

                    def pieces(m):
                        if 1 <= m <= ST:
                            s5_in(m - 1)
                        if 4 <= m < 4 + ST:
                            s5_out(m - 4)
                        if m == 3:
                            sb_scores(0), sb_scores(1)
                        if m == 4:
                            pe.wait_ge(s.evac, layer * PER.evac + SLOT["gg"] + 1)
                            single(banks[:, 2, 0:T], p_("w_gate")[0:16, :], gq[0:16, :]).then_inc(s.gla_z, 1)
                            sb_suffix(0), sb_suffix(1)
                        if m == 5:
                            sb_scores(2), sb_scores(3)
                        if m == 6:
                            sb_suffix(2), sb_suffix(3)
                        if m == 8:
                            pe.wait_ge(s.gla_arg, layer * PER.gla_arg + 1)
                            pe.wait_ge(s.sb_w, layer * PER.sb_w + HEADS)
                            pe.wait_ge(s.evac, layer * PER.evac + SLOT["sbv"] + 1)
                            attend(2, sbv, attA).then_inc(s.sb_o, 1)
                        if m == 9:
                            gla_scores(0), gla_scores(1)
                        if m == 10:
                            gla_scores(2), gla_scores(3)
                        if m == 12:
                            pe.wait_ge(s.gla_attm, layer * PER.gla_attm + HEADS)
                            pe.wait_ge(s.evac, layer * PER.evac + SLOT["gv"] + 1)
                            pe.wait_ge(s.y, layer * PER.y + 1)
                            attend(2, gv, attA).then_inc(s.gla_o, 1)
                            pe.wait_ge(s.dsa_rope, layer * PER.dsa_rope + 1)
                            pe.wait_ge(s.s5_rot, layer * PER.s5_rot + ST)
                            for side in range(2):
                                for pair in range(2):
                                    for tt in range(2):
                                        ins = pe.transpose(
                                            banks[:, 6 + side, pair * T + tt * P:pair * T + (tt + 1) * P],
                                            dqk[:, tt, 4 * side + 2 * pair:4 * side + 2 * pair + 2, :]
                                            .rearrange("p h d -> p (h d)"), c("ident"))
                            ins.then_inc(s.dsa_t, 1)
                        if m == 13:
                            dsa_scores(0), dsa_scores(1)
                        if m == 14:
                            pe.wait_ge(s.gla_sq, layer * PER.gla_sq + 1)
                            single(banks[:, 4, :], c("head_ones"), gn[:, 1, :]).then_inc(s.gla_ss, 1)
                            dsa_scores(2), dsa_scores(3)
                        if m == 15:
                            pe.wait_ge(s.s5_gelu, layer * PER.s5_gelu + 1)
                            pe.wait_ge(s.gla_v, layer * PER.gla_v + 1)
                            for ct in range(4):
                                for k in range(2):
                                    a = PARAM["w_glu"][0] + k * 2 * BW + ct * P
                                    ins = single(banks[:, 4 + ct // 2, (ct % 2) * T:(ct % 2 + 1) * T],
                                                 prm[:, a:a + P], s5g[:, 2, k * T:(k + 1) * T], k == 0 and ct % 2 == 0, k == 1)
                            ins.then_inc(s.s5_glu, 1)
                            dsa_turn(0), dsa_turn(1)
                        if m == 17:
                            dsa_turn(2), dsa_turn(3)
                        if m == 19:
                            pe.wait_ge(s.s5_inner, layer * PER.s5_inner + 1)
                            pe.wait_ge(s.dsa_pte, layer * PER.dsa_pte + HEADS)
                            pe.wait_ge(s.evac, layer * PER.evac + SLOT["dv"] + 1)
                            attend(3, dv, attB).then_inc(s.dsa_o, 1)

                    for m in range(NPROJ + NGATE):
                        b = b0 + m
                        if m >= 2:
                            pe.wait_ge(s.evac, layer * PER.evac + m - 1)
                        if m < NPROJ and PROJ[m] in NATURAL:
                            natural_block(b, b % 3, m % 2)
                        else:
                            in_block(b, b % 3, m % 2, norm=1 if m == 0 else None)
                        pieces(m)

                    for q in range(NBRANCH):
                        b = b0 + NPROJ + NGATE + q
                        block_ready(b)
                        if q == 0:
                            pe.wait_ge(s.b_lo, layer * PER.b_lo + 4)
                        if q == 1:
                            pe.wait_ge(s.evac, layer * PER.evac + NPROJ + NGATE)
                        for dt in range(2):
                            if q >= 2:
                                pe.wait_ge(s.gated, layer * PER.gated + 2 * (q - 2) + dt + 1)
                            for n in range(4):
                                for k in range(2):
                                    last = (dt, n, k) == (1, 3, 1)
                                    bank = (4 if q % 2 == 0 else 0) + 2 * dt + n // 2
                                    inc = s.w_used if last else s.pb_half if (dt, n, k) == (0, 3, 1) else None
                                    three(banks[:, bank, (n % 2) * T:(n % 2 + 1) * T],
                                          w(b % 3, (2 * n + k) * 256 + dt * P, P),
                                          (b_hi[:, n, k, :], b_lo[:, n, k, :]),
                                          k == 0 and n % 2 == 0, last, inc)

                    for o, tiles in enumerate(OUT_TILES):
                        b = b0 + NPROJ + NGATE + NBRANCH + o
                        block_ready(b)
                        if o == 0:
                            pe.wait_ge(s.gated, layer * PER.gated + 5)
                        if o == 2:
                            pe.wait_ge(s.gated, layer * PER.gated + 6)
                        for kt in range(KT):
                            if o == 0:
                                pe.wait_ge(s.m_lo, layer * PER.m_lo + kt + 1)
                            for ct in range(len(tiles)):
                                last = kt == KT - 1 and ct == len(tiles) - 1
                                col = (tiles[ct] % 2) * T
                                three(banks[:, 4 + tiles[ct] // 2, col:col + T],
                                      w(b % 3, kt * P * len(tiles) + ct * P, P), act_tiles(kt),
                                      kt == 0 and col == 0, last, s.w_used if last else None)

                pe.wait_ge(s_params, (layer + 1) * 16)
                sum_squares(0, 6)
                ffn(0, 0)
                sum_squares(1, 6)
                mixer()
                sum_squares(2, 0)
                ffn(1, FFN_BLOCKS + MIX_BLOCKS)

        def ffn_steps(f):
            return (0 if f == 0 else FFN_BLOCKS + MIX_BLOCKS) // RING

        @block.scalar
        def _(act):
            def round_half(layer, k, slot, half):
                if half == 0:
                    act.wait_ge(landed[slot], (layer * (PER_LAYER // RING) + k + 1) * 16)
                    act.wait_ge(s.w_used, layer * PER_LAYER + k * RING + slot + 1)
                a = half * HALF
                act.activation(w_hi[:, slot, a:a + HALF], raw[:, slot, a:a + HALF], ACT.Copy) \
                    .then_inc(s.w_hi, 1)

            def round_weights(layer, k, slot):
                round_half(layer, k, slot, 0)
                round_half(layer, k, slot, 1)

            for slot in range(RING):
                round_weights(0, 0, slot)
            act.wait_ge(s_const, 16)
            with act.Fori(0, LAYERS) as layer:
                own = Steps(act, s.act, layer, PER.act)

                def silu(f, j, buf, k, slot):
                    act.wait_ge(s.w_used, layer * PER.w_used + RING * (k) + slot + 1 + RING)
                    if not (isinstance(j, int) and j < 2):
                        act.wait_ge(s.h_prod, layer * PER.h_prod + FT * f + j - 1)
                    act.activation(a_s[:, buf, :], banks[:, 4 + buf, 0:T], ACT.Silu).then_inc(s.h_silu, 1)

                def hidden_hi(f, j, buf, k=None, slot=None):
                    act.wait_ge(s.h_prod, layer * PER.h_prod + FT * f + j + 1)
                    if k is not None:
                        act.wait_ge(s.w_used, layer * PER.w_used + RING * (k) + slot + 1 + RING)
                    act.activation(h_hi[:, buf, :], hf[:, buf, :], ACT.Copy).then_inc(s.h_hi, 1)

                def norm(n):
                    for q in range(4):
                        act.wait_ge(s.res, layer * PER.res + 4 * n + q + 1)
                        act.activation(U[:, 2 * q:2 * q + 2, :], hT[:, 2 * q:2 * q + 2, :], ACT.Square) \
                            .then_inc(s.sq, 1)
                    act.wait_ge(s.v, layer * PER.v + n + 1)
                    own.link(act.activation(nrm[:, 1, :], nrm[:, 0, :], ACT.Ln))
                    act.activation(nrm[:, 1, :], nrm[:, 1, :], ACT.Exp, scale=-0.5).then_inc(s.y0, 1)
                    if n == 0:
                        act.wait_ge(s_params, (layer + 1) * 16)
                        act.activation(s5n[:, 0, :], p_("log_step"), ACT.Exp).then_inc(s.s5_exp, 1)
                    if n == 1:
                        act.activation(s5n[:, 2, :], s5n[:, 1, :], ACT.Exp).then_inc(s.s5_r, 1)
                    for kt in range(KT):
                        act.wait_ge(s.u, layer * PER.u + 8 * n + kt + 1)
                        act.activation(u_hi[:, kt, :], U[:, kt, :], ACT.Copy).then_inc(s.u_hi, 1)

                def ffn(f):
                    k0 = ffn_steps(f)
                    silu(f, 0, 0, k0, 0)
                    hidden_hi(f, 0, 0)
                    round_weights(layer, k0 + 1, 0)
                    silu(f, 1, 1, k0, 1)
                    hidden_hi(f, 1, 1)
                    round_weights(layer, k0 + 1, 1)

                    def body(i):
                        silu(f, 2 * i, 0, k0 + i - 1, 2)
                        round_weights(layer, k0 + i, 2)
                        hidden_hi(f, 2 * i, 0, k0 + i, 0)
                        round_weights(layer, k0 + i + 1, 0)
                        silu(f, 2 * i + 1, 1, k0 + i, 1)
                        hidden_hi(f, 2 * i + 1, 1)
                        round_weights(layer, k0 + i + 1, 1)

                    body(1)
                    if f == 0:
                        act.wait_ge(s.s5_red, layer * PER.s5_red + 1)
                        own.link(act.activation(s5n[:, 6, :], s5n[:, 5, :], ACT.Abs))
                        act.activation(s5n[:, 7, :], s5n[:, 5, :], ACT.Sin)
                        act.activation(s5n[:, 8, :], s5n[:, 6, :], ACT.Sin, bias=half_pi_c, scale=-1.0) \
                            .then_inc(s.s5_trig, 1)
                    with act.Fori(2, FT // 2) as i:
                        body(i)

                def last_round(f):
                    round_weights(layer, ffn_steps(f) + FT // 2, 2)

                def softplus_parts(h0):
                    for h in (h0, h0 + 1):
                        act.wait_ge(s.sb_z, layer * PER.sb_z + h + 1)
                        if h >= 2:
                            act.wait_ge(s.sb_sp, layer * PER.sb_sp + h - 1)
                    marks = [own.mark(act.activation(sbt[:, h % 2, :], banks[:, 4 + h % 2, 0:ATT], ACT.Abs))
                             for h in (h0, h0 + 1)]
                    for h in (h0, h0 + 1):
                        own.wait(marks[h % 2])
                        marks[h % 2] = own.mark(act.activation(sbt[:, h % 2, :], sbt[:, h % 2, :], ACT.Exp, scale=-1.0))
                    for h in (h0, h0 + 1):
                        own.wait(marks[h % 2])
                        act.activation(sbt[:, h % 2, :], sbt[:, h % 2, :], ACT.Ln, bias=one_c) \
                            .then_inc(s.sb_ln, 1)

                def branch_hi(n, turn, scale):
                    act.wait_ge(s.y, layer * PER.y + turn + 1)
                    act.activation(b_hi[:, n, :, :], yb[:, turn % 2, :, :], ACT.Copy, scale=scale) \
                        .then_inc(s.b_hi, 1)

                targets = {"s5u": s5u, "sbq": sbq, "sbk": sbk, "gqk": gqk, "sbv": sbv, "dv": dv, "gv": gv, "gr": gr}

                def evacuate(m):
                    bank = banks[:, m % 2, :]
                    if m >= NPROJ:
                        g = m - NPROJ
                        if g == NGATE // 2:
                            act.wait_ge(s.s5_state, layer * PER.s5_state + ST)
                        dst = G[:, g // 4, (2 * g) % KT:(2 * g) % KT + 2, :]
                        act.activation(dst, bank, ACT.Tanh, scale=0.5).then_inc(s.evac, 1)
                        return
                    name = PROJ[m]
                    if name == "gg":
                        act.activation(gq[:, :], bank[:, 0:T], ACT.Copy).then_inc(s.evac, 1)
                    elif name in ("dq", "dk"):
                        side = 0 if name == "dq" else 4
                        act.activation(dqk[:, :, side:side + 4, :], bank.rearrange("p (t c) -> p t c", t=2),
                                       ACT.Copy).then_inc(s.evac, 1)
                    else:
                        act.activation(targets[name][:, :, :], bank, ACT.Copy,
                                       scale=0.125 if name == "sbq" else 1.0).then_inc(s.evac, 1)

                def pieces(m):
                    if m in (3, 5):
                        softplus_parts(m - 3)
                    if m in (4, 6):
                        for h in (m - 4, m - 3):
                            act.wait_ge(s.sb_acc, layer * PER.sb_acc + h + 1)
                            act.activation(attA[:, h, :], banks[:, 4 + h % 2, 0:ATT], ACT.Exp) \
                                .then_inc(s.sb_exp, 1)
                    if m == 5:
                        act.wait_ge(s.gla_z, layer * PER.gla_z + 1)
                        own.link(act.activation(gB[:, 0, :], banks[:, 2, 0:T], ACT.Abs, bias=p_("b_gate")))
                        own.link(act.activation(gB[:, 0, :], gB[:, 0, :], ACT.Exp, scale=-1.0))
                        act.activation(gB[:, 0, :], gB[:, 0, :], ACT.Ln, bias=one_c).then_inc(s.gla_ln, 1)
                    if m == 7:
                        act.wait_ge(s.gla_arg, layer * PER.gla_arg + 1)
                        act.activation(kd, kd, ACT.Exp, scale=-1.0 / 16)
                        act.activation(gq[:, :], gq[:, :], ACT.Exp, scale=1.0 / 16).then_inc(s.gla_exp, 1)
                    if m == 8:
                        act.wait_ge(s.gla_kq, layer * PER.gla_kq + 1)
                        act.wait_ge(s.evac, layer * PER.evac + SLOT["dk"] + 1)
                        act.activation(ropeX, dqk[:, :, :, :], ACT.Square).then_inc(s.dsa_sq, 1)
                    if m == 9:
                        branch_hi(0, 0, 1.0)
                        act.wait_ge(s.dsa_ms, layer * PER.dsa_ms + 1)
                        own.link(act.activation(dms[:, 2, :], dms[:, 1, :], ACT.Ln))
                        act.activation(dms[:, 2, :], dms[:, 2, :], ACT.Exp, scale=-0.5).then_inc(s.dsa_y0, 1)
                    if m == 12:
                        act.wait_ge(s.dsa_t, layer * PER.dsa_t + 1)
                        act.activation(dqT, banks[:, 6, :], ACT.Copy, scale=0.125).then_inc(s.dsa_qk, 1)
                    if m == 13:
                        act.wait_ge(s.gla_oc, layer * PER.gla_oc + 1)
                        act.activation(gn[:, 1, :], gn[:, 0, :], ACT.Square).then_inc(s.gla_sq, 1)
                        act.wait_ge(s.evac, layer * PER.evac + SLOT["gr"] + 1)
                        act.activation(gn[:, 2, :], gr[:, :, :].rearrange("p a t -> p (a t)"), ACT.Tanh, scale=0.5) \
                            .then_inc(s.gla_tanh, 1)
                        act.wait_ge(s.s5_inner, layer * PER.s5_inner + 1)
                        act.activation(s5g[:, 1, :], s5g[:, 1, :], ACT.Tanh).then_inc(s.s5_tanh, 1)
                    if m == 15:
                        act.wait_ge(s.gla_v, layer * PER.gla_v + 1)
                        own.link(act.activation(gn[:, 3, :], gn[:, 1, :], ACT.Ln))
                        act.activation(gn[:, 3, :], gn[:, 3, :], ACT.Exp, scale=-0.5).then_inc(s.gla_y0, 1)
                    if m in (13, 15):
                        for h in (m - 13, m - 12):
                            act.wait_ge(s.dsa_max, layer * PER.dsa_max + h + 1)
                            act.activation(attB[:, h, 0:P], attB[:, h, 0:P], ACT.Exp, bias=dmx[:, h, 0:1])
                            act.activation(attB[:, h, P:ATT], attB[:, h, P:ATT], ACT.Exp, bias=dmx[:, h, 1:2]) \
                                .then_inc(s.dsa_exp, 1)
                    if m in (15, 17):
                        for h in (m - 15, m - 14):
                            act.wait_ge(s.dsa_pt, layer * PER.dsa_pt + h + 1)
                            act.activation(attB[:, h, :], banks[:, 6 + h % 2, 0:ATT], ACT.Copy) \
                                .then_inc(s.dsa_pte, 1)
                    if m == 16:
                        act.wait_ge(s.s5_glu, layer * PER.s5_glu + 1)
                        act.activation(s5g[:, 1, :], banks[:, 5, :], ACT.Tanh, scale=0.25).then_inc(s.s5_sig, 1)
                    if m == 17:
                        branch_hi(2, 1, 0.5)
                    if m == 18:
                        branch_hi(1, 2, 0.25)
                    if m == 20:
                        branch_hi(3, 3, 1.0)

                def mixer():
                    k0 = FFN_BLOCKS // RING
                    for m in range(NPROJ + NGATE):
                        act.wait_ge(s.w_used, layer * PER.w_used + RING * (k0 + m // RING) + m % RING + 1 + RING)
                        evacuate(m)
                        round_weights(layer, k0 + m // RING + 1, m % RING)
                        pieces(m)
                    for m in range(NPROJ + NGATE, MIX_BLOCKS - 1):
                        q = m - NPROJ - NGATE
                        for half in range(2):
                            round_half(layer, k0 + m // RING + 1, m % RING, half)
                            if q < NBRANCH:
                                dt = 2 * q + half
                                act.wait_ge(s.mixed, layer * PER.mixed + dt + 1)
                                act.activation(u_hi[:, dt, :], U[:, dt, :], ACT.Copy, scale=0.5) \
                                    .then_inc(s.m_hi, 1)

                norm(0)
                ffn(0)
                norm(1)
                last_round(0)
                mixer()
                norm(2)
                round_weights(layer, (FFN_BLOCKS + MIX_BLOCKS) // RING, 2)
                ffn(1)
                last_round(1)
                assert own.n == PER.act, own.n

        @block.vector
        def _(dve):
            dve.sem_inc(s.w_lo, 2 * RING)

            def half_rest(layer, k, slot, half):
                a = half * HALF
                dve.wait_ge(s.w_hi, layer * PER.w_hi + 2 * (k * RING + slot) + half + 1)
                dve.tensor_tensor(w_lo[:, slot, a:a + HALF], raw[:, slot, a:a + HALF],
                                  w_hi[:, slot, a:a + HALF].bitcast(F32), ALU.subtract).then_inc(s.w_lo, 1)

            def rest_of_weights(layer, k, slot):
                half_rest(layer, k, slot, 0)
                half_rest(layer, k, slot, 1)

            for slot in range(RING):
                rest_of_weights(0, 0, slot)
            dve.wait_ge(s_const, 16)
            dve.wait_ge(s_x, 16)
            dve.sem_inc(s.res, 4)
            with dve.Fori(0, LAYERS) as layer:
                own = Steps(dve, s.dve, layer, PER.dve)

                def newton(v, y, t, o):
                    own.link(dve.tensor_tensor(t, y, y, ALU.mult))
                    own.link(dve.tensor_tensor(t, t, v, ALU.mult))
                    own.link(dve.tensor_scalar(t, t, -0.5, 1.5, ALU.mult, ALU.add))
                    own.link(dve.tensor_tensor(o, y, t, ALU.mult))

                def norm(n):
                    dve.wait_ge(s.ss, layer * PER.ss + n + 1)
                    dve.tensor_scalar(nrm[:, 0, :], banks[:, 0 if n == 2 else 6, 0:T], -1.0 / D, EPS,
                                      ALU.mult, ALU.add).then_inc(s.v, 1)
                    dve.wait_ge(s.y0, layer * PER.y0 + n + 1)
                    newton(nrm[:, 0, :], nrm[:, 1, :], nrm[:, 2, :], nrm[:, 3, :])
                    gain = p_(("g_ffn1", "g_mix", "g_ffn2")[n])
                    for kt in range(KT):
                        dve.scalar_tensor_tensor(out=U[:, kt, :], in0=hT[:, kt, :], scalar=gain[:, kt:kt + 1],
                                                 in1=nrm[:, 3, :], op0=ALU.mult, op1=ALU.mult).then_inc(s.u, 1)

                def reduce_angles():
                    N = lambda i: s5n[:, i, :]
                    dve.wait_ge(s.s5_exp, layer * PER.s5_exp + 1)
                    dve.tensor_tensor(N(1), p_("lam_re"), N(0), ALU.mult)
                    own.link(dve.tensor_tensor(N(3), p_("lam_im"), N(0), ALU.mult))
                    own.link(dve.tensor_scalar(N(4), N(3), 1.0 / TWO_PI, ROUND, ALU.mult, ALU.add))
                    own.link(dve.tensor_scalar(N(4), N(4), -ROUND, None, ALU.add))
                    at = 3
                    for part in (PI_A, PI_B, PI_C):
                        own.link(dve.scalar_tensor_tensor(out=N(5), in0=N(4), scalar=-part, in1=N(at),
                                                          op0=ALU.mult, op1=ALU.add))
                        at = 5
                    dve.tensor_scalar(N(5), N(5), PI_BELOW, -PI_BELOW, ALU.min, ALU.max).then_inc(s.s5_red, 1)
                    own.mark(dve.tensor_tensor(N(9), p_("lam_re"), p_("lam_re"), ALU.mult))
                    own.link(dve.tensor_tensor(N(10), p_("lam_im"), p_("lam_im"), ALU.mult))
                    own.link(dve.tensor_tensor(N(9), N(9), N(10), ALU.add))
                    dve.reciprocal(N(10), N(9)).then_inc(s.s5_rden, 1)

                def product(f, j, buf):
                    dve.wait_ge(s.h_silu, layer * PER.h_silu + FT * f + j + 1)
                    dve.tensor_tensor(hf[:, buf, :], banks[:, 4 + buf, T:2 * T], a_s[:, buf, :], ALU.mult) \
                        .then_inc(s.h_prod, 1)

                def hidden_lo(f, j, buf):
                    dve.wait_ge(s.h_hi, layer * PER.h_hi + FT * f + j + 1)
                    dve.tensor_tensor(h_lo[:, buf, :], hf[:, buf, :], h_hi[:, buf, :].bitcast(F32), ALU.subtract) \
                        .then_inc(s.h_lo, 1)

                def ffn(f):
                    k0 = ffn_steps(f)
                    product(f, 0, 0)
                    hidden_lo(f, 0, 0)
                    rest_of_weights(layer, k0 + 1, 0)
                    product(f, 1, 1)
                    hidden_lo(f, 1, 1)
                    rest_of_weights(layer, k0 + 1, 1)

                    def body(i):
                        product(f, 2 * i, 0)
                        rest_of_weights(layer, k0 + i, 2)
                        hidden_lo(f, 2 * i, 0)
                        rest_of_weights(layer, k0 + i + 1, 0)
                        product(f, 2 * i + 1, 1)
                        hidden_lo(f, 2 * i + 1, 1)
                        rest_of_weights(layer, k0 + i + 1, 1)

                    body(1)
                    with dve.Fori(2, FT // 2) as i:
                        body(i)
                    for q in range(4):
                        if q < 3:
                            dve.wait_ge(s.ffn_acc, layer * PER.ffn_acc + 3 * f + q + 1)
                        else:
                            dve.wait_ge(s.w_used, layer * PER.w_used + RING * (k0 + FT // 2 - 1) + 2 + 1 + RING)
                        dve.scalar_tensor_tensor(out=hT[:, 2 * q:2 * q + 2, :].rearrange("p a t -> p (a t)"),
                                                 in0=banks[:, q, :], scalar=0.5,
                                                 in1=hT[:, 2 * q:2 * q + 2, :].rearrange("p a t -> p (a t)"),
                                                 op0=ALU.mult, op1=ALU.add).then_inc(s.res, 1)

                def last_rest(f):
                    rest_of_weights(layer, ffn_steps(f) + FT // 2, 2)

                def s5_rotate(i):
                    dve.wait_ge(s.s5_p, layer * PER.s5_p + i + 1)
                    if i == 0:
                        dve.wait_ge(s.s5_tab, layer * PER.s5_tab + 1)
                    if i >= 2:
                        dve.wait_ge(s.s5_state, layer * PER.s5_state + i - 1)
                    bank = banks[:, 6 + i % 2, :].rearrange("p (c t) -> p c t", c=2)
                    x = s5x[:, i % 2, :, :, :]
                    dve.tensor_tensor(x[:, 0, 0, :], bank[:, 0, :], rotC[:, i, :], ALU.mult)
                    dve.tensor_tensor(x[:, 0, 1, :], bank[:, 1, :], rotC[:, i, :], ALU.mult)
                    dve.tensor_tensor(x[:, 1, 0, :], bank[:, 1, :], rotS[:, i, :], ALU.mult)
                    dve.tensor_tensor(x[:, 1, 1, :], bank[:, 0, :], rotS[:, i, :], ALU.mult).then_inc(s.s5_rot, 1)

                def s5_scan(i):
                    dve.wait_ge(s.s5_x, layer * PER.s5_x + i + 1)
                    decay = s5n[:, 2, i:i + 1].to_broadcast([P, T])
                    for part in range(2):
                        ins = dve.tensor_tensor_scan(s5x[:, i % 2, 1, part, :], decay, s5x[:, i % 2, 0, part, :],
                                                     0.0, ALU.mult, ALU.add)
                    ins.then_inc(s.s5_scan, 1)

                def branch_lo(n, turn, scale):
                    dve.wait_ge(s.b_hi, layer * PER.b_hi + turn + 1)
                    dve.scalar_tensor_tensor(out=b_lo[:, n, :, :], in0=yb[:, turn % 2, :, :], scalar=scale,
                                             in1=b_hi[:, n, :, :].bitcast(F32), op0=ALU.mult, op1=ALU.subtract) \
                        .then_inc(s.b_lo, 1)

                def dilated_softmax(h):
                    dve.wait_ge(s.dsa_s, layer * PER.dsa_s + h + 1)
                    own.link(dve.tensor_tensor(attB[:, h, :], banks[:, 6 + h % 2, 0:ATT], c("forbid"), ALU.add))
                    dve.tensor_reduce(dmx[:, h, 0:1], attB[:, h, 0:P], AX.X, ALU.max, negate=True)
                    dve.tensor_reduce(dmx[:, h, 1:2], attB[:, h, P:ATT], AX.X, ALU.max, negate=True) \
                        .then_inc(s.dsa_max, 1)

                def dilated_weights(h):
                    dve.wait_ge(s.dsa_exp, layer * PER.dsa_exp + h + 1)
                    count = c("count")
                    dve.tensor_tensor_reduce(attB[:, h, 0:P], attB[:, h, 0:P], count[:, 0:P], 1.0, 0.0,
                                             ALU.mult, ALU.add, dmx[:, h, 2:3])
                    own.link(dve.tensor_tensor_reduce(attB[:, h, P:ATT], attB[:, h, P:ATT], count[:, P:ATT], 1.0, 0.0,
                                                      ALU.mult, ALU.add, dmx[:, h, 3:4]))
                    own.link(dve.reciprocal(dmx[:, h, 4:6], dmx[:, h, 2:4]))
                    dve.tensor_scalar(attB[:, h, 0:P], attB[:, h, 0:P], dmx[:, h, 4:5], None, ALU.mult)
                    dve.tensor_scalar(attB[:, h, P:ATT], attB[:, h, P:ATT], dmx[:, h, 5:6], None, ALU.mult) \
                        .then_inc(s.dsa_p, 1)

                def gla_mask(h):
                    dve.wait_ge(s.gla_att, layer * PER.gla_att + h + 1)
                    dve.scalar_tensor_tensor(out=attA[:, h, :], in0=banks[:, 4 + h % 2, 0:ATT], scalar=3e38,
                                             in1=c("causal"), op0=ALU.min, op1=ALU.mult).then_inc(s.gla_attm, 1)

                def pieces(m):
                    if 1 <= m <= ST:
                        s5_scan(m - 1)
                    if m in (3, 5):
                        for h in (m - 3, m - 2):
                            dve.wait_ge(s.sb_ln, layer * PER.sb_ln + h + 1)
                            own.link(dve.scalar_tensor_tensor(out=attA[:, h, :], in0=banks[:, 4 + h % 2, 0:ATT],
                                                              scalar=0.0, in1=sbt[:, h % 2, :], op0=ALU.max,
                                                              op1=ALU.add))
                            dve.tensor_tensor(attA[:, h, :], attA[:, h, :], c("strict"), ALU.mult) \
                                .then_inc(s.sb_sp, 1)
                    if m in (4, 6):
                        for h in (m - 4, m - 3):
                            dve.wait_ge(s.sb_exp, layer * PER.sb_exp + h + 1)
                            dve.scalar_tensor_tensor(out=attA[:, h, :], in0=attA[:, h, :], scalar=3e38,
                                                     in1=c("strict"), op0=ALU.min, op1=ALU.mult) \
                                .then_inc(s.sb_w, 1)
                    if m == 5:
                        dve.wait_ge(s.gla_ln, layer * PER.gla_ln + 1)
                        own.link(dve.tensor_scalar(gB[:, 1, :], banks[:, 2, 0:T], p_("b_gate"), 0.0, ALU.add, ALU.min))
                        own.link(dve.tensor_tensor(gB[:, 1, :], gB[:, 1, :], gB[:, 0, :], ALU.subtract))
                        own.link(dve.tensor_tensor_scan(gB[:, 2, :], one_c.to_broadcast([P, T]), gB[:, 1, :], 0.0,
                                                        ALU.mult, ALU.add))
                    if m == 7:
                        for i in range(NGC):
                            at, n = (P * i, P) if i < 4 else (P * 4 + T * (i - 4), T)
                            mid = gB[:, 2, GC * i + GC // 2 - 1:GC * i + GC // 2]
                            dve.tensor_scalar(kd[:, at:at + n], gB[:, 2, 0:n], mid, -GLA_CLIP, ALU.subtract, ALU.max)
                            ins = dve.tensor_scalar(gq[:, GC * i:GC * i + GC], gB[:, 2, GC * i:GC * i + GC], mid,
                                                    GLA_CLIP, ALU.subtract, ALU.min)
                        ins.then_inc(s.gla_arg, 1)
                        dve.wait_ge(s.gla_exp, layer * PER.gla_exp + 1)
                        near = kd[:, 0:4 * P].rearrange("p (i t) -> p i t", i=4)
                        far = kd[:, 4 * P:6 * T].rearrange("p (i t) -> p i t", i=4)
                        dve.tensor_tensor(near, near, gqk[:, 1, 0:P].unsqueeze(1).to_broadcast([P, 4, P]), ALU.mult)
                        dve.tensor_tensor(far, far, gqk[:, 1, :].unsqueeze(1).to_broadcast([P, 4, T]), ALU.mult)
                        dve.scalar_tensor_tensor(out=gq[:, :], in0=gq[:, :], scalar=float(32 ** -0.5),
                                                 in1=gqk[:, 0, :], op0=ALU.mult, op1=ALU.mult) \
                            .then_inc(s.gla_kq, 1)
                    if m == 8:
                        dve.wait_ge(s.sb_o, layer * PER.sb_o + 1)
                        dve.tensor_copy(yb[:, 0, :, :].rearrange("p a t -> p (a t)"), banks[:, 2, :]) \
                            .then_inc(s.y, 1)
                    if m == 9:
                        gla_mask(0), gla_mask(1)
                        dve.wait_ge(s.dsa_sq, layer * PER.dsa_sq + 1)
                        own.link(dve.tensor_reduce(dms[:, 0, :], ropeX.rearrange("p t h d -> p (t h) d"),
                                                   AX.X, ALU.add))
                        dve.tensor_scalar(dms[:, 1, :], dms[:, 0, :], 1.0 / 64, EPS, ALU.mult, ALU.add) \
                            .then_inc(s.dsa_ms, 1)
                    if m == 10:
                        gla_mask(2), gla_mask(3)
                        branch_lo(0, 0, 1.0)
                        dve.wait_ge(s.dsa_y0, layer * PER.dsa_y0 + 1)
                        newton(dms[:, 1, :], dms[:, 2, :], dms[:, 3, :], dms[:, 4, :])
                        flat = dqk[:, :, :, :].rearrange("p t h d -> p (t h) d")
                        own.link(dve.tensor_tensor(flat, flat, dms[:, 4, :].unsqueeze(2).to_broadcast([P, 16, 64]),
                                                   ALU.mult))
                        a = PARAM["dsa_gain"][0]
                        for side in range(2):
                            gain = prm[:, a + 64 * side:a + 64 * side + 64]
                            x = dqk[:, :, 4 * side:4 * side + 4, :]
                            n = own.mark(dve.tensor_tensor(
                                x, x, gain.unsqueeze(1).unsqueeze(1).to_broadcast([P, 2, 4, 64]), ALU.mult))
                        own.wait(n)
                    if m == 11:
                        for tt in range(2):
                            x = dqk[:, tt, :, :]
                            sin = c("sin")[:, 64 * tt:64 * tt + 64].unsqueeze(1).to_broadcast([P, 8, 64])
                            dve.tensor_tensor(ropeX[:, tt, :, 0:32], x[:, :, 32:64], sin[:, :, 0:32], ALU.mult)
                            n = own.mark(dve.tensor_tensor(ropeX[:, tt, :, 32:64], x[:, :, 0:32], sin[:, :, 32:64],
                                                           ALU.mult))
                        own.wait(n)
                        for tt in range(2):
                            x = dqk[:, tt, :, :]
                            cos = c("cos")[:, 64 * tt:64 * tt + 64].unsqueeze(1).to_broadcast([P, 8, 64])
                            n = own.mark(dve.tensor_tensor(x, x, cos, ALU.mult))
                        own.wait(n)
                        dve.tensor_tensor(dqk[:, :, :, :], dqk[:, :, :, :], ropeX, ALU.add).then_inc(s.dsa_rope, 1)
                    if m == 12:
                        dve.wait_ge(s.gla_o, layer * PER.gla_o + 1)
                        dve.tensor_copy(gn[:, 0, :], banks[:, 2, :]).then_inc(s.gla_oc, 1)
                        dve.wait_ge(s.dsa_t, layer * PER.dsa_t + 1)
                        dve.tensor_copy(dkT, banks[:, 7, :]).then_inc(s.dsa_qk, 1)
                        dve.wait_ge(s.s5_y, layer * PER.s5_y + ST)
                        for k in range(2):
                            n = own.mark(dve.scalar_tensor_tensor(
                                out=s5g[:, 0, k * T:(k + 1) * T], in0=s5u[:, k, :], scalar=p_("s5_d")[:, k:k + 1],
                                in1=banks[:, 3, k * T:(k + 1) * T], op0=ALU.mult, op1=ALU.add))
                        own.wait(n)
                        own.link(dve.tensor_tensor(s5g[:, 1, :], s5g[:, 0, :], s5g[:, 0, :], ALU.mult))
                        root = math.sqrt(2 / math.pi)
                        own.link(dve.tensor_scalar(s5g[:, 1, :], s5g[:, 1, :], 0.044715 * root, root,
                                                   ALU.mult, ALU.add))
                        dve.tensor_tensor(s5g[:, 1, :], s5g[:, 1, :], s5g[:, 0, :], ALU.mult) \
                            .then_inc(s.s5_inner, 1)
                    if m == 13:
                        dilated_softmax(0), dilated_softmax(1)
                    if m == 14:
                        dve.wait_ge(s.gla_ss, layer * PER.gla_ss + 1)
                        dve.tensor_scalar(gn[:, 1, :], banks[:, 4, :], 1.0 / 64, EPS, ALU.mult, ALU.add) \
                            .then_inc(s.gla_v, 1)
                        dve.wait_ge(s.s5_tanh, layer * PER.s5_tanh + 1)
                        dve.scalar_tensor_tensor(out=s5g[:, 2, :], in0=s5g[:, 1, :], scalar=1.0, in1=s5g[:, 0, :],
                                                 op0=ALU.add, op1=ALU.mult).then_inc(s.s5_gelu, 1)
                        dilated_weights(0), dilated_weights(1)
                        dilated_softmax(2), dilated_softmax(3)
                    if m == 15:
                        dve.wait_ge(s.gla_tanh, layer * PER.gla_tanh + 1)
                        own.link(dve.scalar_tensor_tensor(out=gn[:, 2, :], in0=gn[:, 2, :], scalar=1.0,
                                                          in1=gr[:, :, :].rearrange("p a t -> p (a t)"),
                                                          op0=ALU.add, op1=ALU.mult))
                    if m == 16:
                        dilated_weights(2), dilated_weights(3)
                        dve.wait_ge(s.gla_y0, layer * PER.gla_y0 + 1)
                        t = yb[:, 1, :, :].rearrange("p a t -> p (a t)")
                        newton(gn[:, 1, :], gn[:, 3, :], t, gn[:, 3, :])
                        own.link(dve.tensor_tensor(gn[:, 0, :], gn[:, 0, :], gn[:, 3, :], ALU.mult))
                        for k in range(2):
                            ins = dve.scalar_tensor_tensor(
                                out=yb[:, 1, k, :], in0=gn[:, 0, k * T:(k + 1) * T], scalar=p_("gla_norm")[:, k:k + 1],
                                in1=gn[:, 2, k * T:(k + 1) * T], op0=ALU.mult, op1=ALU.mult)
                        ins.then_inc(s.y, 1)
                    if m == 17:
                        dve.wait_ge(s.b_lo, layer * PER.b_lo + 1)
                        dve.wait_ge(s.s5_sig, layer * PER.s5_sig + 1)
                        dve.scalar_tensor_tensor(out=yb[:, 0, :, :].rearrange("p a t -> p (a t)"),
                                                 in0=s5g[:, 1, :], scalar=1.0, in1=banks[:, 4, :],
                                                 op0=ALU.add, op1=ALU.mult).then_inc(s.y, 1)
                    if m == 18:
                        branch_lo(2, 1, 0.5)
                    if m == 19:
                        branch_lo(1, 2, 0.25)
                        dve.wait_ge(s.b_lo, layer * PER.b_lo + 2)
                        dve.wait_ge(s.dsa_o, layer * PER.dsa_o + 1)
                        dve.tensor_copy(yb[:, 1, :, :].rearrange("p a t -> p (a t)"), banks[:, 3, :]) \
                            .then_inc(s.y, 1)
                    if m == 21:
                        branch_lo(3, 3, 1.0)

                def gate(dt):
                    q = dt // 2
                    if dt % 2 == 0:
                        dve.wait_ge(s.pb_half, layer * PER.pb_half + q + 1)
                    else:
                        k = NPROJ + NGATE + q
                        dve.wait_ge(s.w_used, layer * PER.w_used + RING * ((FFN_BLOCKS + k) // RING) + (FFN_BLOCKS + k) % RING + 1 + RING)
                    if dt == 0:
                        dve.wait_ge(s.evac, layer * PER.evac + NPROJ + NGATE)
                    if dt >= 2:
                        dve.wait_ge(s.mixed, layer * PER.mixed + dt - 1)
                    bank = (4 if q % 2 == 0 else 0) + 2 * (dt % 2)
                    dve.scalar_tensor_tensor(
                        out=prods[dt % 2], in0=G[:, :, dt, :], scalar=1.0,
                        in1=banks[:, bank:bank + 2, :].rearrange("p b (n t) -> p (b n) t", n=2),
                        op0=ALU.add, op1=ALU.mult).then_inc(s.gated, 1)

                def mixed_lo(dt):
                    dve.wait_ge(s.m_hi, layer * PER.m_hi + dt + 1)
                    dve.scalar_tensor_tensor(out=u_lo[:, dt, :], in0=U[:, dt, :], scalar=0.5,
                                             in1=u_hi[:, dt, :].bitcast(F32), op0=ALU.mult, op1=ALU.subtract) \
                        .then_inc(s.m_lo, 1)

                def mixer():
                    k0 = FFN_BLOCKS // RING
                    for m in range(NPROJ + NGATE):
                        if 1 <= m <= ST:
                            s5_rotate(m - 1)
                        rest_of_weights(layer, k0 + m // RING + 1, m % RING)
                        pieces(m)
                    for q in range(NBRANCH):
                        m = NPROJ + NGATE + q
                        gate(2 * q)
                        if q > 0:
                            mixed_lo(2 * q - 2)
                        half_rest(layer, k0 + m // RING + 1, m % RING, 0)
                        gate(2 * q + 1)
                        if q > 0:
                            mixed_lo(2 * q - 1)
                        half_rest(layer, k0 + m // RING + 1, m % RING, 1)
                    mixed_lo(6)
                    mixed_lo(7)
                    for o, tiles in enumerate(OUT_TILES):
                        m = NPROJ + NGATE + NBRANCH + o
                        q = tiles[0] // 2
                        if o != 3:
                            dve.wait_ge(s.w_used, layer * PER.w_used + RING * (k0 + m // RING) + m % RING + 1 + RING)
                            x = hT[:, 2 * q:2 * q + 2, :].rearrange("p a t -> p (a t)")
                            dve.tensor_tensor(x, banks[:, 4 + q, :], x, ALU.add).then_inc(s.res, 1)
                        if o < 4:
                            rest_of_weights(layer, k0 + m // RING + 1, m % RING)

                dve.wait_ge(s_params, (layer + 1) * 16)
                norm(0)
                reduce_angles()
                ffn(0)
                norm(1)
                last_rest(0)
                mixer()
                norm(2)
                rest_of_weights(layer, (FFN_BLOCKS + MIX_BLOCKS) // RING, 2)
                ffn(1)
                last_rest(1)
                assert own.n == PER.dve, own.n

        @block.gpsimd
        def _(pool):
            pool.wait_ge(s_const, 16)
            with pool.Fori(0, LAYERS) as layer:
                own = Steps(pool, s.pool, layer, PER.pool)

                def tt(o, a, b, op):
                    own.link(pool.tensor_tensor(o, a, b, op))

                def norm(n):
                    for kt in range(KT):
                        pool.wait_ge(s.u_hi, layer * PER.u_hi + 8 * n + kt + 1)
                        pool.tensor_tensor(u_lo[:, kt, :], U[:, kt, :], u_hi[:, kt, :].bitcast(F32), ALU.subtract) \
                            .then_inc(s.u_lo, 1)

                N = lambda i: s5n[:, i, :]

                def const(i, shape=(P, ST)):
                    return c("scalars")[:, i:i + 1].to_broadcast(list(shape))

                one, zero, minus_half, three_halves = (const(i) for i in (2, 3, 4, 5))

                def unit(cn, sn):
                    tt(N(11), N(cn), N(cn), ALU.mult)
                    tt(N(12), N(sn), N(sn), ALU.mult)
                    tt(N(11), N(11), N(12), ALU.add)
                    tt(N(11), N(11), minus_half, ALU.mult)
                    tt(N(11), N(11), three_halves, ALU.add)
                    tt(N(cn), N(cn), N(11), ALU.mult)
                    tt(N(sn), N(sn), N(11), ALU.mult)

                def rotations():
                    pool.wait_ge(s.s5_trig, layer * PER.s5_trig + 1)
                    tt(rotC[:, :, 0], one, one, ALU.mult)
                    tt(rotS[:, :, 0], one, one, ALU.subtract)
                    tt(N(13), N(8), one, ALU.mult)
                    tt(N(14), N(7), one, ALU.mult)
                    unit(13, 14)
                    w = 1
                    while w < T:
                        ta = tabA[:, 0:ST * w].rearrange("p (i t) -> p i t", i=ST)
                        tb = tabB[:, 0:ST * w].rearrange("p (i t) -> p i t", i=ST)
                        cz = N(13).unsqueeze(2).to_broadcast([P, ST, w])
                        sz = N(14).unsqueeze(2).to_broadcast([P, ST, w])
                        tt(ta, rotC[:, :, 0:w], cz, ALU.mult)
                        tt(tb, rotS[:, :, 0:w], sz, ALU.mult)
                        tt(rotC[:, :, w:2 * w], ta, tb, ALU.subtract)
                        tt(ta, rotC[:, :, 0:w], sz, ALU.mult)
                        tt(tb, rotS[:, :, 0:w], cz, ALU.mult)
                        if 2 * w == T:
                            pool.tensor_tensor(rotS[:, :, w:2 * w], ta, tb, ALU.add).then_inc(s.s5_tab, 1)
                        else:
                            tt(rotS[:, :, w:2 * w], ta, tb, ALU.add)
                        if 2 * w < T:
                            tt(N(15), N(13), N(13), ALU.mult)
                            tt(N(16), N(14), N(14), ALU.mult)
                            tt(N(17), N(13), N(14), ALU.mult)
                            tt(N(13), N(15), N(16), ALU.subtract)
                            tt(N(14), N(17), N(17), ALU.add)
                            unit(13, 14)
                        w *= 2

                def coefficients():
                    pool.wait_ge(s.s5_r, layer * PER.s5_r + 1)
                    pool.wait_ge(s.s5_rden, layer * PER.s5_rden + 1)
                    tt(N(19), N(2), N(8), ALU.mult)
                    tt(N(19), N(19), one, ALU.subtract)
                    tt(N(20), N(2), N(7), ALU.mult)
                    tt(N(11), N(19), p_("lam_re"), ALU.mult)
                    tt(N(12), N(20), p_("lam_im"), ALU.mult)
                    tt(N(21), N(11), N(12), ALU.add)
                    tt(N(21), N(21), N(10), ALU.mult)
                    tt(N(11), N(20), p_("lam_re"), ALU.mult)
                    tt(N(12), N(19), p_("lam_im"), ALU.mult)
                    tt(N(22), N(11), N(12), ALU.subtract)
                    tt(N(22), N(22), N(10), ALU.mult)
                    tt(N(23), zero, N(21), ALU.subtract)
                    tt(N(24), zero, N(22), ALU.subtract)
                    a = PARAM["s5_c"][0]
                    c_re = prm[:, a:a + ST * 32].rearrange("p (i h) -> p i h", i=ST)
                    c_im = prm[:, a + ST * 32:a + 2 * ST * 32].rearrange("p (i h) -> p i h", i=ST)
                    t = tabA[:, 0:ST * 32].rearrange("p (i h) -> p i h", i=ST)
                    wide = lambda i: N(i).unsqueeze(2).to_broadcast([P, ST, 32])
                    tt(t, c_im, wide(24), ALU.mult)
                    tt(s5c[:, 0, :, :], c_re, wide(21), ALU.mult)
                    tt(s5c[:, 0, :, :], s5c[:, 0, :, :], t, ALU.add)
                    tt(t, c_im, wide(23), ALU.mult)
                    tt(s5c[:, 1, :, :], c_re, wide(24), ALU.mult)
                    pool.tensor_tensor(s5c[:, 1, :, :], s5c[:, 1, :, :], t, ALU.add).then_inc(s.s5_coef, 1)

                def s5_tile(i):
                    x = s5x[:, i % 2, :, :, :]
                    pool.wait_ge(s.s5_rot, layer * PER.s5_rot + i + 1)
                    n = own.mark(pool.tensor_tensor(x[:, 0, 0, :], x[:, 0, 0, :], x[:, 1, 0, :], ALU.add))
                    pool.tensor_tensor(x[:, 0, 1, :], x[:, 0, 1, :], x[:, 1, 1, :], ALU.subtract) \
                        .then_inc(s.s5_x, 1)
                    own.wait(n)
                    pool.wait_ge(s.s5_scan, layer * PER.s5_scan + i + 1)
                    if i >= 2:
                        pool.wait_ge(s.s5_y, layer * PER.s5_y + i - 1)
                    own.mark(pool.tensor_tensor(x[:, 0, 0, :], x[:, 1, 0, :], rotC[:, i, :], ALU.mult))
                    own.mark(pool.tensor_tensor(x[:, 0, 1, :], x[:, 1, 1, :], rotC[:, i, :], ALU.mult))
                    re, im = st[:, i % 2, 0, :], st[:, i % 2, 1, :]
                    own.mark(pool.tensor_tensor(re, x[:, 1, 1, :], rotS[:, i, :], ALU.mult))
                    own.link(pool.tensor_tensor(im, x[:, 1, 0, :], rotS[:, i, :], ALU.mult))
                    tt(re, x[:, 0, 0, :], re, ALU.subtract)
                    pool.tensor_tensor(im, x[:, 0, 1, :], im, ALU.add).then_inc(s.s5_state, 1)

                def mix(dt):
                    pool.wait_ge(s.gated, layer * PER.gated + dt + 1)
                    p = prods[dt % 2]
                    tt(p[:, 0:2, :], p[:, 0:2, :], p[:, 2:4, :], ALU.add)
                    pool.tensor_tensor(U[:, dt, :], p[:, 0, :], p[:, 1, :], ALU.add).then_inc(s.mixed, 1)

                pool.wait_ge(s_params, (layer + 1) * 16)
                norm(0)
                rotations()
                norm(1)
                coefficients()
                for i in range(ST):
                    s5_tile(i)
                for dt in range(KT):
                    mix(dt)
                norm(2)
                assert own.n == PER.pool, own.n

    return nc


def _constants():
    k = np.zeros((P, NCONST), np.float32)

    def put(name, a):
        at, n = CONST[name]
        k[:, at:at + n] = np.asarray(a, np.float32).reshape(P, n)

    r = np.arange(P)
    put("ident", np.eye(P))
    put("head_ones", (r[:, None] // 64 == r[None, :] // 64))
    put("neg_suffix", -(r[:, None] >= r[None, :]).astype(np.float32))
    put("neg_ones", -np.ones((P, P)))
    key = np.concatenate([np.tile(r[:, None], (1, T)), np.tile(r[:, None] + P, (1, P))], 1)
    query = np.concatenate([np.tile(np.arange(T), (P, 1)), np.tile(np.arange(P, T), (P, 1))], 1)
    put("causal", key <= query)
    put("strict", key < query)
    query = np.concatenate([np.tile(r[:, None], (1, P)), np.tile(r[:, None] + P, (1, T))], 1)
    key = np.concatenate([np.tile(r, (P, 1)), np.tile(np.arange(T), (P, 1))], 1)
    gap = query - key
    count = np.zeros((P, ATT), np.float32)
    for window, dil in ((128, 1), (512, 4), (2048, 16)):
        count += (gap >= 0) & (gap % dil == 0) & (gap // dil <= window // dil)
    put("count", count)
    put("forbid", np.where(count > 0, 0.0, -1e30))
    inv = np.float32(10000.0) ** (-np.arange(0, 64, 2, dtype=np.float32) / np.float32(64))
    ang = (np.arange(T, dtype=np.float32)[:, None] * inv[None, :].astype(np.float32)).astype(np.float64)
    cos, sin = np.cos(ang), np.sin(ang)
    both = lambda a, b: np.concatenate([a, b], 1).reshape(2, P, 64).transpose(1, 0, 2)
    put("cos", both(cos, cos))
    put("sin", both(-sin, sin))
    put("scalars", np.tile(np.array([EPS, math.pi / 2, 1.0, 0.0, -0.5, 1.5]), (P, 1)))
    return k


def _rows(w):
    return w.reshape(w.shape[0] // P, P, w.shape[1]).transpose(1, 0, 2)


def _stream(ffn1_w_in, ffn1_w_out, w_in, w_branch, w_out, ffn2_w_in, ffn2_w_out):
    s = np.zeros((LAYERS * PER_LAYER + RING, P, BLK), np.float32)

    def ffn(at, w_i, w_o):
        a = _rows(w_i).reshape(P, KT, 2, FT, P).transpose(3, 0, 1, 2, 4).reshape(FT, P, BLK)
        o = w_o.reshape(FT // 2, 2, P, D).transpose(0, 2, 1, 3).reshape(FT // 2, P, BLK)
        s[at], s[at + 1] = a[0], a[1]
        for i in range(1, FT // 2):
            s[at + 3 * i - 1], s[at + 3 * i], s[at + 3 * i + 1] = a[2 * i], o[i - 1], a[2 * i + 1]
        s[at + FFN_BLOCKS - 1] = o[-1]

    first = {"sbq": 0, "sbk": 256, "sbv": 512, "s5u": 768, "gqk": 1024, "gv": 1280, "gr": 1536, "gg": 1792,
             "dq": 1808, "dk": 2064, "dv": 2320}
    gates = 2576
    for layer in range(LAYERS):
        at = layer * PER_LAYER
        ffn(at, ffn1_w_in[layer], ffn1_w_out[layer])
        at += FFN_BLOCKS
        rows = _rows(w_in[layer])
        for name in PROJ:
            if name == "gg":
                s[at].reshape(P, KT, 256)[:, :, 0:16] = rows[:, :, 1792:1808]
            else:
                s[at] = rows[:, :, first[name]:first[name] + 256].reshape(P, BLK)
            at += 1
        for g in range(NGATE):
            s[at] = rows[:, :, gates + 256 * g:gates + 256 * (g + 1)].reshape(P, BLK)
            at += 1
        rows = w_branch[layer].reshape(4, 2, P, D).transpose(2, 0, 1, 3).reshape(P, 8, D)
        for q in range(NBRANCH):
            s[at] = rows[:, :, 256 * q:256 * (q + 1)].reshape(P, BLK)
            at += 1
        rows = _rows(w_out[layer])
        for tiles in OUT_TILES:
            n = len(tiles) * P
            s[at][:, 0:KT * n] = rows[:, :, tiles[0] * P:tiles[0] * P + n].reshape(P, KT * n)
            at += 1
        ffn(at, ffn2_w_in[layer], ffn2_w_out[layer])
    return s


def _params(i):
    k = np.zeros((LAYERS + 1, P, NPARAM), np.float32)
    for layer in range(LAYERS):
        def put(name, a):
            at, n = PARAM[name]
            k[layer, 0:a.shape[0], at:at + n] = a.reshape(a.shape[0], n)

        tiles = lambda a: a.reshape(-1, P).T
        put("g_ffn1", tiles(i["ffn1_norm"][layer]))
        put("g_mix", tiles(i["mix_norm"][layer]))
        put("g_ffn2", tiles(i["ffn2_norm"][layer]))
        put("gla_norm", tiles(i["gla_norm"][layer]))
        put("b_gate", tiles(i["gla_b_gate"][layer]))
        put("s5_d", tiles(i["s5_d"][layer].reshape(-1)))
        put("lam_re", tiles(i["s5_lam_re"][layer].reshape(-1)))
        put("lam_im", tiles(i["s5_lam_im"][layer].reshape(-1)))
        put("log_step", tiles(np.repeat(i["s5_log_step"][layer], 64)))
        put("dsa_gain", np.broadcast_to(np.concatenate([i["dsa_q_norm"][layer], i["dsa_k_norm"][layer]]), (P, 128)))
        put("w_gate", i["gla_w_gate"][layer])
        b = np.zeros((2, 2, P, P), np.float32)
        c = np.zeros((2, P, ST, 32), np.float32)
        for part, (bm, cm) in enumerate([("s5_b_re", "s5_c_re"), ("s5_b_im", "s5_c_im")]):
            for g in range(16):
                t, e = g // 2, g % 2
                b[part, t // 4, 32 * (t % 4) + 16 * e:32 * (t % 4) + 16 * e + 16, 64 * e:64 * e + 64] = \
                    i[bm][layer][g].T
                c[part, 64 * e:64 * e + 64, t, 16 * e:16 * e + 16] = i[cm][layer][g].T
        put("s5_b", b.transpose(2, 0, 1, 3))
        put("s5_c", c.transpose(1, 0, 2, 3))
        put("w_glu", _rows(i["s5_w_glu"][layer]))
    return k


def kernel(**inputs):
    import concourse.bacc as _bacc
    from concourse.bass_utils import run_bass_kernel_spmd as _run

    i = {name: np.asarray(a) for name, a in inputs.items()}
    arrays = {
        "x_t": np.ascontiguousarray(_rows(i["x"][0].T)),
        "weights": _stream(i["ffn1_w_in"], i["ffn1_w_out"], i["w_in"], i["w_branch"], i["w_out"],
                           i["ffn2_w_in"], i["ffn2_w_out"]),
        "params": _params(i),
        "constants": _constants(),
    }
    nc = _bacc.Bacc("TRN2", target_bir_lowering=False, num_devices=1, dynamic_dma_scratch_size=1024)
    args = [nc.dram_tensor(n, a.shape, F32, kind="ExternalInput").ap() for n, a in arrays.items()]
    args.append(nc.dram_tensor("out_t", (P, KT, T), F32, kind="ExternalOutput").ap())
    build(nc, *args)
    r = _run(nc, [arrays], core_ids=[0])
    return r.results[0]["out_t"].transpose(1, 0, 2).reshape(D, T).T.reshape(1, T, D)
```

```python
import math
from contextlib import ExitStack

import numpy as np

import concourse.bass as bass
from concourse import mybir

F32 = mybir.dt.float32
F32R = mybir.dt.float32r
ACT = mybir.ActivationFunctionType
ALU = mybir.AluOpType
AX = mybir.AxisListType

P = 128
LAYERS = 2
T = 256
D = 1024
KT = D // P
DFF = 2816
FT = DFF // P
BW = 256
HEADS = 4
EPS = 1e-6

BLK = 2048
HALF = BLK // 2
RING = 3
FFN_BLOCKS = FT + FT // 2
PROJ = ["s5u", "sbq", "sbk", "gg", "dq", "dk", "gqk", "sbv", "dv", "gv", "gr"]
NPROJ = len(PROJ)
NGATE = 16
NBRANCH = 4
OUT_TILES = [(0, 1), (2, 3), (4, 5), (6,), (7,)]
MIX_BLOCKS = NPROJ + NGATE + NBRANCH + len(OUT_TILES)
PER_LAYER = 2 * FFN_BLOCKS + MIX_BLOCKS
assert PER_LAYER % RING == 0 and FFN_BLOCKS % RING == 0 and MIX_BLOCKS % RING == 0
NATURAL = {"dq", "dk", "sbv", "dv", "gv"}
SLOT = {name: m for m, name in enumerate(PROJ)}
BY_ACT = [m < NPROJ and PROJ[m] in NATURAL for m in range(NPROJ + NGATE)]
NTH = [sum(b == BY_ACT[m] for b in BY_ACT[:m + 1]) for m in range(NPROJ + NGATE)]

ATT = T + P

GC = 32
NGC = T // GC
GLA_CLIP = 85.0 * 16

STATES = 1024
ST = STATES // P

CONST = {}
_at = 0
for _name, _n in [("ident", P), ("head_ones", P), ("neg_suffix", P), ("neg_ones", P),
                  ("causal", ATT), ("strict", ATT), ("count", T), ("forbid", T),
                  ("cos", 2 * 64), ("sin", 2 * 64), ("scalars", 6)]:
    CONST[_name] = (_at, _n)
    _at += _n
NCONST = _at

PARAM = {}
_at = 0
for _name, _n in [("g_ffn1", KT), ("g_mix", KT), ("g_ffn2", KT), ("gla_norm", 2), ("b_gate", 1),
                  ("s5_d", 2), ("lam_re", ST), ("lam_im", ST), ("log_step", ST),
                  ("dsa_gain", 2 * 64), ("w_gate", P), ("s5_b", 2 * 2 * P), ("s5_c", 2 * ST * 32),
                  ("w_glu", 2 * 2 * BW)]:
    PARAM[_name] = (_at, _n)
    _at += _n
NPARAM = _at
NGAIN = 3 * KT

class PER:
    w_hi = 2 * PER_LAYER
    w_lo = 2 * PER_LAYER
    w_used = PER_LAYER
    h_ab = 2 * FT
    h_silu = 2 * FT
    h_prod = 2 * FT
    h_hi = 2 * FT
    h_lo = 2 * FT
    ffn_acc = 6
    res = 12
    sq = 12
    sq_add = 6
    sq_sum = 3
    ss = 3
    v = 3
    y0 = 3
    rstd = 3
    u = 12
    u_hi = 12
    u_lo = 12
    evac_v = NPROJ - len(NATURAL) + NGATE
    evac_a = len(NATURAL)
    tanh = NGATE
    s5_exp = 1
    s5_red = 1
    s5_trig = 1
    s5_tab = 1
    s5_r = 1
    s5_rden = 1
    s5_coef = 1
    s5_p = ST
    s5_rot = ST
    s5_x = ST
    s5_scan = ST
    s5_state = ST
    s5_y = ST
    s5_inner = 1
    s5_tanh = 1
    s5_gelu = 1
    s5_glu = 1
    s5_sig = 1
    sb_z = HEADS
    sb_ln = HEADS
    sb_sp = HEADS
    sb_acc = HEADS
    sb_exp = HEADS
    sb_w = HEADS
    sb_o = 1
    gla_z = 1
    gla_ln = 1
    gla_zread = 1
    gla_arg = 1
    gla_exp = 1
    gla_kq = 1
    gla_att = HEADS
    gla_attm = HEADS
    gla_o = 1
    gla_oc = 1
    gla_sq = 1
    gla_ss = 1
    gla_v = 1
    gla_y0 = 1
    gla_tanh = 1
    dsa_sq = 1
    dsa_ms = 1
    dsa_y0 = 1
    dsa_rope = 1
    dsa_t = 1
    dsa_qk = 2
    dsa_s = HEADS
    dsa_max = HEADS
    dsa_exp = HEADS
    dsa_p = HEADS
    dsa_pt = HEADS
    dsa_pte = HEADS
    dsa_o = 1
    y = 4
    b_hi = 4
    b_lo = 4
    pb_half = 4
    gated = 8
    mixed = 8
    m_hi = 8
    m_lo = 8
    dve = 62
    act = 16
    pool = 216


class Signals:
    pass


TWO_PI = 2 * math.pi
PI_A = 6.28125
PI_B = float(np.float32(TWO_PI - PI_A))
PI_C = float(TWO_PI - PI_A - PI_B)
ROUND = 1.5 * 2.0 ** 23
PI_BELOW = 3.14159250259


class Steps:

    def __init__(self, eng, sem, layer, per):
        self.eng, self.sem, self.layer, self.per, self.n = eng, sem, layer, per, 0

    def mark(self, ins):
        ins.then_inc(self.sem, 1)
        self.n += 1
        return self.n

    def wait(self, n):
        self.eng.wait_ge(self.sem, self.layer * self.per + n)

    def link(self, ins):
        self.wait(self.mark(ins))


def build(nc, x_in, stream, params_in, const_in, out):
    ctx = ExitStack()
    with ctx:
        def sb(name, shape, dt=F32):
            return ctx.enter_context(nc.sbuf_tensor(name, shape, dt))

        def sem(name):
            return ctx.enter_context(nc.semaphore(name))

        raw = sb("raw", [P, RING, BLK])
        w_hi = sb("w_hi_t", [P, RING, BLK], F32R)
        w_lo = sb("w_lo_t", [P, RING, BLK], F32R)
        hT = sb("hT", [P, KT, T])
        U = sb("U", [P, KT, T])
        u_hi = sb("u_hi_t", [P, KT, T], F32R)
        u_lo = sb("u_lo_t", [P, KT, T], F32R)
        G = sb("G", [P, 4, KT, T])
        b_hi = sb("b_hi_t", [P, 4, 2, T], F32R)
        b_lo = sb("b_lo_t", [P, 4, 2, T], F32R)
        h_hi = sb("h_hi_t", [P, 2, T], F32R)
        h_lo = sb("h_lo_t", [P, 2, T], F32R)
        cst = sb("cst", [P, NCONST])
        prm = sb("prm", [P, NPARAM])
        yb = sb("yb", [P, 2, 2, T])
        attA = sb("attA", [P, HEADS, ATT])
        attB = sb("attB", [P, HEADS, ATT])
        s5u = sb("s5u", [P, 2, T])
        s5x = sb("s5x", [P, 2, 2, 2, T])
        st = sb("st", [P, 2, 2, T])
        s5n = sb("s5n", [P, 25, ST])
        s5c = sb("s5c", [P, 2, ST, 32])
        sbqk = sb("sbqk", [P, 2, 2, T])
        sbv = sb("sbv", [P, 2, T])
        gqk = sb("gqk", [P, 2, T])
        gq = sb("gq", [P, T])
        dqk = sb("dqk", [P, 2, 8, 64])
        dv = sb("dv", [P, 2, T])
        rstd_mix = sb("rstd_mix", [P, T + 2])
        dms = sb("dms", [P, 5, 16])
        dmx = sb("dmx", [P, HEADS, 6])

        rotC, rotS = G[:, 2, :, :], G[:, 3, :, :]
        squares = [yb[:, 0, :, :], yb[:, 1, :, :], sbqk[:, 0, :, :], sbqk[:, 1, :, :]]
        flat = lambda x: x.rearrange("p a t -> p (a t)")
        n_v, n_y, n_t = flat(squares[1]), flat(squares[2]), flat(squares[3])
        rstd_ffn = gq[:, :]
        ab, hf = sbqk, yb[:, :, 0, :]
        tiles8 = lambda x: x.rearrange("p n k t -> p (n k) t")
        in_hi = [u_hi[:, :, :], tiles8(b_hi[:, :, :, :])]
        in_lo = [u_lo[:, :, :], tiles8(b_lo[:, :, :, :])]
        end_hi = [x[:, 6:8, :] for x in (in_hi[1], in_hi[0])]
        end_lo = [x[:, 6:8, :] for x in (in_lo[1], in_lo[0])]
        sbq, sbk = sbqk[:, 0, :, :], sbqk[:, 1, :, :]
        gv, gr = sbqk[:, 0, :, :], sbqk[:, 1, :, :]
        sbt = attB[:, 0:2, :]
        gB = attB[:, 2:4, :].rearrange("p h c -> p (h c)").rearrange("p (k t) -> p k t", k=3)
        kd = U[:, 0:6, :].rearrange("p a t -> p (a t)")
        gn = U[:, :, :].rearrange("p (k a) t -> p k (a t)", k=4)
        ropeX = attB[:, :, :].rearrange("p h c -> p (h c)")[:, 0:2 * 8 * 64] \
            .rearrange("p (t h d) -> p t h d", t=2, h=8)
        dqT = dqk[:, 0, :, :].rearrange("p h d -> p (h d)")
        dkT = dqk[:, 1, :, :].rearrange("p h d -> p (h d)")
        s5g = s5x[:, :, :, :, :].rearrange("p a b c t -> p (a b) (c t)")
        prods = [attA[:, :, 0:T], attB[:, :, 0:T]]
        tabA = attA[:, :, :].rearrange("p h c -> p (h c)")
        tabB = attB[:, :, :].rearrange("p h c -> p (h c)")

        banks = ctx.enter_context(nc.psum_tensor("banks", [P, 8, 512], F32))

        landed = [sem(f"landed{i}") for i in range(RING)]
        s = Signals()
        s.w_hi = sem("w_hi")
        s.w_lo = sem("w_lo")
        s.w_used = sem("w_used")
        s.h_ab = sem("h_ab")
        s.h_silu = sem("h_silu")
        s.h_prod = sem("h_prod")
        s.h_hi = sem("h_hi")
        s.h_lo = sem("h_lo")
        s.ffn_acc = sem("ffn_acc")
        s.res = sem("res")
        s.sq = sem("sq")
        s.sq_sum = sem("sq_sum")
        s.sq_add = sem("sq_add")
        s.ss = sem("ss")
        s.v = sem("v")
        s.y0 = sem("y0")
        s.rstd = sem("rstd")
        s.u = sem("u")
        s.u_hi = sem("u_hi")
        s.u_lo = sem("u_lo")
        s.evac_v = sem("evac_v")
        s.evac_a = sem("evac_a")
        s.tanh = sem("tanh")
        s.s5_exp = sem("s5_exp")
        s.s5_red = sem("s5_red")
        s.s5_trig = sem("s5_trig")
        s.s5_tab = sem("s5_tab")
        s.s5_r = sem("s5_r")
        s.s5_rden = sem("s5_rden")
        s.s5_coef = sem("s5_coef")
        s.s5_p = sem("s5_p")
        s.s5_rot = sem("s5_rot")
        s.s5_x = sem("s5_x")
        s.s5_scan = sem("s5_scan")
        s.s5_state = sem("s5_state")
        s.s5_y = sem("s5_y")
        s.s5_inner = sem("s5_inner")
        s.s5_tanh = sem("s5_tanh")
        s.s5_gelu = sem("s5_gelu")
        s.s5_glu = sem("s5_glu")
        s.s5_sig = sem("s5_sig")
        s.sb_z = sem("sb_z")
        s.sb_ln = sem("sb_ln")
        s.sb_sp = sem("sb_sp")
        s.sb_acc = sem("sb_acc")
        s.sb_exp = sem("sb_exp")
        s.sb_w = sem("sb_w")
        s.sb_o = sem("sb_o")
        s.gla_z = sem("gla_z")
        s.gla_ln = sem("gla_ln")
        s.gla_zread = sem("gla_zread")
        s.gla_arg = sem("gla_arg")
        s.gla_exp = sem("gla_exp")
        s.gla_kq = sem("gla_kq")
        s.gla_att = sem("gla_att")
        s.gla_attm = sem("gla_attm")
        s.gla_o = sem("gla_o")
        s.gla_oc = sem("gla_oc")
        s.gla_sq = sem("gla_sq")
        s.gla_ss = sem("gla_ss")
        s.gla_v = sem("gla_v")
        s.gla_y0 = sem("gla_y0")
        s.gla_tanh = sem("gla_tanh")
        s.dsa_sq = sem("dsa_sq")
        s.dsa_ms = sem("dsa_ms")
        s.dsa_y0 = sem("dsa_y0")
        s.dsa_rope = sem("dsa_rope")
        s.dsa_t = sem("dsa_t")
        s.dsa_qk = sem("dsa_qk")
        s.dsa_s = sem("dsa_s")
        s.dsa_max = sem("dsa_max")
        s.dsa_exp = sem("dsa_exp")
        s.dsa_p = sem("dsa_p")
        s.dsa_pt = sem("dsa_pt")
        s.dsa_pte = sem("dsa_pte")
        s.dsa_o = sem("dsa_o")
        s.y = sem("y")
        s.b_hi = sem("b_hi")
        s.b_lo = sem("b_lo")
        s.pb_half = sem("pb_half")
        s.gated = sem("gated")
        s.mixed = sem("mixed")
        s.m_hi = sem("m_hi")
        s.m_lo = sem("m_lo")
        s.dve = sem("dve")
        s.act = sem("act")
        s.pool = sem("pool")
        s_x = [sem("x_landed0"), sem("x_landed1")]
        s_gain = sem("gains_landed")
        s_const = sem("const_landed")
        s_params = sem("params_landed")
        s_out = sem("out_stored")

        def c(name, rows=P):
            a, n = CONST[name]
            return cst[0:rows, a:a + n]

        def p_(name):
            a, n = PARAM[name]
            return prm[:, a:a + n]

        eps_c, half_pi_c, one_c = (c("scalars")[:, i:i + 1] for i in range(3))

        block = ctx.enter_context(nc.Block())

        @block.sync
        def _(sp):
            def load(n, slot):
                sp.dma_start(raw[:, slot, :], stream[n]).then_inc(landed[slot], 16)

            sp.dma_start(prm[:, 0:NGAIN], params_in[0][:, 0:NGAIN]).then_inc(s_gain, 16)
            sp.dma_start(hT[:, 0:4, :], x_in[:, 0:4, :]).then_inc(s_x[0], 16)
            sp.dma_start(hT[:, 4:8, :], x_in[:, 4:8, :]).then_inc(s_x[1], 16)
            load(0, 0)
            load(1, 1)
            sp.dma_start(cst[:, :], const_in).then_inc(s_const, 16)
            load(2, 2)
            sp.dma_start(prm[:, NGAIN:NPARAM], params_in[0][:, NGAIN:NPARAM]).then_inc(s_params, 16)
            with sp.Fori(0, LAYERS) as layer:
                def next_three(n0):
                    for slot in range(RING):
                        sp.wait_ge(s.w_lo, layer * PER.w_lo + 2 * n0 + 2 * slot + 2)
                        load(layer * PER_LAYER + n0 + slot, slot)

                with sp.Fori(0, (FFN_BLOCKS + MIX_BLOCKS) // RING) as t:
                    next_three(t * RING + RING)
                sp.wait_ge(s.u, layer * PER.u + 12)
                sp.dma_start(prm[:, :], params_in[layer + 1]).then_inc(s_params, 16)
                with sp.Fori((FFN_BLOCKS + MIX_BLOCKS) // RING, PER_LAYER // RING) as t:
                    next_three(t * RING + RING)
            for q in range(4):
                sp.wait_ge(s.res, (LAYERS - 1) * PER.res + 8 + q + 1)
                sp.dma_start(out[:, 2 * q:2 * q + 2, :], hT[:, 2 * q:2 * q + 2, :]).then_inc(s_out, 16)
            sp.wait_ge(s_out, 4 * 16)
            sp.wait_ge(s_params, (LAYERS + 1) * 16)

        @block.tensor
        def _(pe):
            pe.sem_inc(s.w_used, RING)

            def three(o, st, mv, start, stop, inc=None):
                pe.matmul(o, st[0], mv[0], start=start, stop=False, skip_group_check=True)
                pe.matmul(o, st[0], mv[1], start=False, stop=False, skip_group_check=True)
                ins = pe.matmul(o, st[1], mv[0], start=False, stop=stop, skip_group_check=True)
                if inc is not None:
                    ins.then_inc(inc, 1)

            def w(slot, a, n):
                return w_hi[:, slot, a:a + n], w_lo[:, slot, a:a + n]

            def act_tiles(kt, a=0, n=T, where=0):
                return in_hi[where][:, kt, a:a + n], in_lo[where][:, kt, a:a + n]

            def single(o, st, mv, start=True, stop=True):
                return pe.matmul(o, st, mv, start=start, stop=stop, skip_group_check=True)

            with pe.Fori(0, LAYERS) as layer:
                def block_ready(b):
                    pe.wait_ge(s.w_lo, layer * PER.w_lo + 2 * b + 8)

                def in_block(b, slot, bank, norm=None, where=0):
                    block_ready(b)
                    for kt in range(KT):
                        if norm is not None:
                            pe.wait_ge(s.u_lo, layer * PER.u_lo + 4 * norm + kt // 2 + 1)
                        for ct in range(2):
                            last = kt == KT - 1 and ct == 1
                            three(banks[:, bank, ct * T:(ct + 1) * T], w(slot, kt * 256 + ct * P, P),
                                  act_tiles(kt, where=where), kt == 0 and ct == 0, last, s.w_used if last else None)

                def natural_block(b, slot, bank):
                    block_ready(b)
                    for kt in range(KT):
                        for tt in range(2):
                            last = kt == KT - 1 and tt == 1
                            three(banks[:, bank, tt * BW:(tt + 1) * BW], act_tiles(kt, tt * P, P),
                                  w(slot, kt * 256, 256), kt == 0 and tt == 0, last,
                                  s.w_used if last else None)

                def sum_squares(norm):
                    pe.wait_ge(s_const, 16)
                    pe.wait_ge(s.sq_sum, layer * PER.sq_sum + norm + 1)
                    for k in range(2):
                        ins = single(banks[:, 7, 0:T], c("neg_ones"), squares[0][:, k, :], k == 0, k == 1)
                    if norm == 1:
                        for tt in range(2):
                            for k in range(2):
                                ins = single(banks[:, 7, T + tt:T + tt + 1], squares[0][:, k, tt * P:(tt + 1) * P],
                                             c("neg_ones")[:, 0:1], False, k == 1)
                    ins.then_inc(s.ss, 1)

                def ffn(f, b0):
                    def out_block(i, b, slot, tiles_first, hi=h_hi, lo=h_lo):
                        block_ready(b)
                        pe.wait_ge(s.h_lo, layer * PER.h_lo + FT * f + 2 * i + 2)
                        order = [(dt, k) for dt in range(KT) for k in range(2)] if tiles_first else \
                                [(dt, k) for k in range(2) for dt in range(KT)]
                        for dt, k in order:
                            first = isinstance(i, int) and i == 0 and k == 0
                            o = banks[:, dt // 2, (dt % 2) * T:(dt % 2 + 1) * T]
                            last = (dt, k) == order[-1]
                            three(o, w(slot, k * D + dt * P, P), (hi[:, k, :], lo[:, k, :]),
                                  first and dt % 2 == 0, False, s.w_used if last else
                                  (s.ffn_acc if tiles_first and k == 1 and dt % 2 == 1 else None))

                    in_block(b0, b0 % 3, 4, norm=0 if f == 0 else 2, where=f)
                    sum_squares(0 if f == 0 else 2)
                    in_block(b0 + 1, (b0 + 1) % 3, 5, where=f)

                    def body(i, first):
                        if first:
                            in_block(b0 + 2, (b0 + 2) % 3, 6, where=f)
                        else:
                            pe.wait_ge(s.h_ab, layer * PER.h_ab + FT * f + 2 * i - 1)
                            in_block(b0 + 3 * i - 1, (b0 + 2) % 3, 4, where=f)
                        out_block(0 if first else i - 1, b0 + 3 * i, b0 % 3, False)
                        pe.wait_ge(s.h_ab, layer * PER.h_ab + FT * f + 2 * i)
                        in_block(b0 + 3 * i + 1, (b0 + 1) % 3, 5, where=f)

                    body(1, True)
                    with pe.Fori(2, FT // 2 - 1) as i:
                        body(i, False)
                    pe.wait_ge(s.h_ab, layer * PER.h_ab + FT * f + FT - 3)
                    in_block(b0 + FFN_BLOCKS - 4, (b0 + 2) % 3, 4, where=f)
                    pe.wait_ge(s.h_ab, layer * PER.h_ab + FT * f + FT - 2)
                    in_block(b0 + FFN_BLOCKS - 3, b0 % 3, 5, where=f)
                    out_block(FT // 2 - 2, b0 + FFN_BLOCKS - 2, (b0 + 1) % 3, False)
                    out_block(FT // 2 - 1, b0 + FFN_BLOCKS - 1, (b0 + 2) % 3, True, end_hi[f], end_lo[f])

                def mixer():
                    b0 = FFN_BLOCKS
                    head = lambda t, h, a, n: t[64 * (h % 2):64 * (h % 2) + 64, h // 2, a:a + n]

                    def scores(o_bank, k, q, h):
                        single(banks[:, o_bank, 0:T], head(k, h, 0, P), head(q, h, 0, T))
                        return single(banks[:, o_bank, T:ATT], head(k, h, P, P), head(q, h, P, P), start=False)

                    def attend(bank, v, att):
                        for h in range(HEADS):
                            o = banks[64 * (h % 2):64 * (h % 2) + 64, bank, (h // 2) * T:(h // 2 + 1) * T]
                            single(o, v[:, 0, 64 * h:64 * h + 64], att[:, h, 0:T], h < 2, False)
                            ins = single(o[:, P:T], v[:, 1, 64 * h:64 * h + 64], att[:, h, T:ATT], False, True)
                        return ins

                    def s5_in(i):
                        if i == 0:
                            pe.wait_ge(s.evac_v, layer * PER.evac_v + NTH[SLOT["s5u"]])
                        if i >= 2:
                            pe.wait_ge(s.s5_rot, layer * PER.s5_rot + i - 1)
                        q = 32 * (i % 4)
                        for part in range(2):
                            a = PARAM["s5_b"][0] + (part * 2 + i // 4) * P
                            ins = single(banks[:, 6 + i % 2, part * T:(part + 1) * T], prm[q:q + 32, a:a + P],
                                         s5u[q:q + 32, i // 4, :], part == 0, True)
                        ins.then_inc(s.s5_p, 1)

                    def s5_out(i):
                        pe.wait_ge(s.s5_state, layer * PER.s5_state + i + 1)
                        if i == 0:
                            pe.wait_ge(s.s5_coef, layer * PER.s5_coef + 1)
                        q = 32 * (i % 4)
                        o = banks[q:q + 32, 3, (i // 4) * T:(i // 4 + 1) * T]
                        single(o, s5c[:, 0, i, :], st[:, i % 2, 0, :], i < 4, False)
                        single(o, s5c[:, 1, i, :], st[:, i % 2, 1, :], False, True).then_inc(s.s5_y, 1)

                    def sb_scores(h):
                        pe.wait_ge(s.evac_v, layer * PER.evac_v + NTH[SLOT["sbk"]])
                        if h >= 2:
                            pe.wait_ge(s.sb_exp, layer * PER.sb_exp + h - 1)
                        scores(4 + h % 2, sbk, sbq, h).then_inc(s.sb_z, 1)

                    def sb_suffix(h):
                        pe.wait_ge(s.sb_sp, layer * PER.sb_sp + h + 1)
                        bank = 4 + h % 2
                        single(banks[:, bank, 0:T], c("neg_suffix"), attA[:, h, 0:T], False, False)
                        single(banks[:, bank, P:T], c("neg_ones"), attA[:, h, T:ATT], False, False)
                        single(banks[:, bank, T:ATT], c("neg_suffix"), attA[:, h, T:ATT], False, True) \
                            .then_inc(s.sb_acc, 1)

                    def gla_scores(h):
                        pe.wait_ge(s.gla_kq, layer * PER.gla_kq + 1)
                        pe.wait_ge(s.sb_exp, layer * PER.sb_exp + HEADS)
                        if h >= 2:
                            pe.wait_ge(s.gla_attm, layer * PER.gla_attm + h - 1)
                        r = slice(32 * h, 32 * h + 32)
                        first = True
                        for i in range(NGC):
                            at = P * i if i < 4 else P * 4 + T * (i - 4)
                            for jt in range(1 if i < 4 else 2):
                                col = GC * i if jt == 0 else T + GC * i - P
                                ins = single(banks[:, 4 + h % 2, col:col + GC], kd[r, at + jt * P:at + (jt + 1) * P],
                                             gq[r, GC * i:GC * i + GC], first, True)
                                first = False
                        ins.then_inc(s.gla_att, 1)

                    def dsa_scores(h):
                        pe.wait_ge(s.dsa_qk, layer * PER.dsa_qk + 2)
                        if h >= 2:
                            pe.wait_ge(s.dsa_max, layer * PER.dsa_max + h - 1)
                        hd = lambda t, a, n: t[64 * (h % 2):64 * (h % 2) + 64, (h // 2) * T + a:(h // 2) * T + a + n]
                        single(banks[:, 6 + h % 2, 0:P], hd(dqT, 0, P), hd(dkT, 0, P))
                        single(banks[:, 6 + h % 2, P:ATT], hd(dqT, P, P), hd(dkT, 0, T), False) \
                            .then_inc(s.dsa_s, 1)

                    def dsa_turn(h):
                        pe.wait_ge(s.dsa_p, layer * PER.dsa_p + h + 1)
                        if h < 2:
                            pe.wait_ge(s.dsa_max, layer * PER.dsa_max + h + 3)
                        else:
                            pe.wait_ge(s.dsa_pte, layer * PER.dsa_pte + h - 1)
                        for j in range(3):
                            ins = pe.transpose(banks[:, 6 + h % 2, j * P:(j + 1) * P], attB[:, h, j * P:(j + 1) * P],
                                               c("ident"))
                        ins.then_inc(s.dsa_pt, 1)

                    def pieces(m):
                        if 1 <= m <= ST:
                            s5_in(m - 1)
                        if 4 <= m < 4 + ST:
                            s5_out(m - 4)
                        if m == 3:
                            sb_scores(0), sb_scores(1)
                        if m == 4:
                            pe.wait_ge(s.evac_v, layer * PER.evac_v + NTH[SLOT["gg"]])
                            single(banks[:, 2, 0:T], p_("w_gate")[0:16, :], gq[0:16, :]).then_inc(s.gla_z, 1)
                            sb_suffix(0), sb_suffix(1)
                        if m == 5:
                            sb_scores(2), sb_scores(3)
                        if m == 6:
                            sb_suffix(2), sb_suffix(3)
                        if m == 8:
                            pe.wait_ge(s.gla_zread, layer * PER.gla_zread + 1)
                            pe.wait_ge(s.sb_w, layer * PER.sb_w + HEADS)
                            pe.wait_ge(s.evac_a, layer * PER.evac_a + NTH[SLOT["sbv"]])
                            attend(2, sbv, attA).then_inc(s.sb_o, 1)
                        if m == 9:
                            gla_scores(0), gla_scores(1)
                        if m == 10:
                            gla_scores(2), gla_scores(3)
                        if m == 12:
                            pe.wait_ge(s.gla_attm, layer * PER.gla_attm + HEADS)
                            pe.wait_ge(s.evac_a, layer * PER.evac_a + NTH[SLOT["gv"]])
                            pe.wait_ge(s.y, layer * PER.y + 1)
                            attend(2, gv, attA).then_inc(s.gla_o, 1)
                            pe.wait_ge(s.dsa_rope, layer * PER.dsa_rope + 1)
                            pe.wait_ge(s.s5_rot, layer * PER.s5_rot + ST)
                            for side in range(2):
                                for pair in range(2):
                                    for tt in range(2):
                                        ins = pe.transpose(
                                            banks[:, 6 + side, pair * T + tt * P:pair * T + (tt + 1) * P],
                                            dqk[:, tt, 4 * side + 2 * pair:4 * side + 2 * pair + 2, :]
                                            .rearrange("p h d -> p (h d)"), c("ident"))
                            ins.then_inc(s.dsa_t, 1)
                        if m == 13:
                            dsa_scores(0), dsa_scores(1)
                        if m == 14:
                            pe.wait_ge(s.gla_sq, layer * PER.gla_sq + 1)
                            single(banks[:, 4, :], c("head_ones"), gn[:, 1, :]).then_inc(s.gla_ss, 1)
                            dsa_scores(2), dsa_scores(3)
                        if m == 15:
                            pe.wait_ge(s.s5_gelu, layer * PER.s5_gelu + 1)
                            pe.wait_ge(s.gla_v, layer * PER.gla_v + 1)
                            for ct in range(4):
                                for k in range(2):
                                    a = PARAM["w_glu"][0] + k * 2 * BW + ct * P
                                    ins = single(banks[:, 4 + ct // 2, (ct % 2) * T:(ct % 2 + 1) * T],
                                                 prm[:, a:a + P], s5g[:, 2, k * T:(k + 1) * T], k == 0 and ct % 2 == 0, k == 1)
                            ins.then_inc(s.s5_glu, 1)
                            dsa_turn(0), dsa_turn(1)
                        if m == 17:
                            dsa_turn(2), dsa_turn(3)
                        if m == 19:
                            pe.wait_ge(s.s5_inner, layer * PER.s5_inner + 1)
                            pe.wait_ge(s.dsa_pte, layer * PER.dsa_pte + HEADS)
                            pe.wait_ge(s.evac_a, layer * PER.evac_a + NTH[SLOT["dv"]])
                            attend(3, dv, attB).then_inc(s.dsa_o, 1)

                    for m in range(NPROJ + NGATE):
                        b = b0 + m
                        if m >= 2 and BY_ACT[m - 2]:
                            pe.wait_ge(s.evac_a, layer * PER.evac_a + NTH[m - 2])
                        elif m >= 2:
                            pe.wait_ge(s.evac_v, layer * PER.evac_v + NTH[m - 2])
                        if m < NPROJ and PROJ[m] in NATURAL:
                            natural_block(b, b % 3, m % 2)
                        else:
                            in_block(b, b % 3, m % 2, norm=1 if m == 0 else None)
                        if m == 0:
                            sum_squares(1)
                        pieces(m)

                    for q in range(NBRANCH):
                        b = b0 + NPROJ + NGATE + q
                        block_ready(b)
                        if q == 0:
                            pe.wait_ge(s.b_lo, layer * PER.b_lo + 4)
                        if q == 1:
                            pe.wait_ge(s.evac_v, layer * PER.evac_v + NTH[-1])
                        for dt in range(2):
                            if q >= 2:
                                pe.wait_ge(s.gated, layer * PER.gated + 2 * (q - 2) + dt + 1)
                            for n in range(4):
                                for k in range(2):
                                    last = (dt, n, k) == (1, 3, 1)
                                    bank = (4 if q % 2 == 0 else 0) + 2 * dt + n // 2
                                    inc = s.w_used if last else s.pb_half if (dt, n, k) == (0, 3, 1) else None
                                    three(banks[:, bank, (n % 2) * T:(n % 2 + 1) * T],
                                          w(b % 3, (2 * n + k) * 256 + dt * P, P),
                                          (b_hi[:, n, k, :], b_lo[:, n, k, :]),
                                          k == 0 and n % 2 == 0, last, inc)

                    for o, tiles in enumerate(OUT_TILES):
                        b = b0 + NPROJ + NGATE + NBRANCH + o
                        block_ready(b)
                        if o == 0:
                            pe.wait_ge(s.gated, layer * PER.gated + 5)
                        if o == 2:
                            pe.wait_ge(s.gated, layer * PER.gated + 6)
                        for kt in range(KT):
                            if o == 0:
                                pe.wait_ge(s.m_lo, layer * PER.m_lo + kt + 1)
                            for ct in range(len(tiles)):
                                last = kt == KT - 1 and ct == len(tiles) - 1
                                col = (tiles[ct] % 2) * T
                                three(banks[:, 4 + tiles[ct] // 2, col:col + T],
                                      w(b % 3, kt * P * len(tiles) + ct * P, P), act_tiles(kt),
                                      kt == 0 and col == 0, last, s.w_used if last else None)

                ffn(0, 0)
                pe.wait_ge(s_params, (layer + 1) * 16)
                mixer()
                ffn(1, FFN_BLOCKS + MIX_BLOCKS)

        def ffn_steps(f):
            return (0 if f == 0 else FFN_BLOCKS + MIX_BLOCKS) // RING

        @block.scalar
        def _(act):
            def round_half(layer, k, slot, half):
                if half == 0:
                    act.wait_ge(landed[slot], (layer * (PER_LAYER // RING) + k + 1) * 16)
                    act.wait_ge(s.w_used, layer * PER_LAYER + k * RING + slot + 1)
                a = half * HALF
                act.activation(w_hi[:, slot, a:a + HALF], raw[:, slot, a:a + HALF], ACT.Copy) \
                    .then_inc(s.w_hi, 1)

            def round_weights(layer, k, slot):
                round_half(layer, k, slot, 0)
                round_half(layer, k, slot, 1)

            def split_pair(done, q, where=0):
                act.wait_ge(s.u, done + q + 1)
                act.activation(in_hi[where][:, 2 * q:2 * q + 2, :], U[:, 2 * q:2 * q + 2, :], ACT.Copy).then_inc(s.u_hi, 1)

            def square_pair(done, q):
                act.wait_ge(s.u, done + q + 1)
                act.activation(squares[q], hT[:, 2 * q:2 * q + 2, :], ACT.Square).then_inc(s.sq, 1)

            split_pair(0, 0)
            split_pair(0, 1)
            round_weights(0, 0, 0)
            split_pair(0, 2)
            split_pair(0, 3)
            for q in range(4):
                square_pair(0, q)
            round_weights(0, 0, 1)
            round_weights(0, 0, 2)
            act.wait_ge(s_const, 16)
            with act.Fori(0, LAYERS) as layer:
                own = Steps(act, s.act, layer, PER.act)

                def silu(f, j, buf):
                    act.wait_ge(s.h_ab, layer * PER.h_ab + FT * f + j + 1)
                    act.activation(ab[:, buf, 0, :], ab[:, buf, 0, :], ACT.Silu).then_inc(s.h_silu, 1)

                def hidden_hi(f, j, buf, k=None, slot=None, hi=h_hi):
                    act.wait_ge(s.h_prod, layer * PER.h_prod + FT * f + j + 1)
                    if k is not None:
                        act.wait_ge(s.w_used, layer * PER.w_used + RING * (k) + slot + 1 + RING)
                    act.activation(hi[:, buf, :], hf[:, buf, :], ACT.Copy).then_inc(s.h_hi, 1)

                def norm(n):
                    width = T + 2 if n == 1 else T
                    act.wait_ge(s.v, layer * PER.v + n + 1)
                    own.link(act.activation(n_y[:, 0:width], n_v[:, 0:width], ACT.Ln))
                    act.activation(n_y[:, 0:width], n_y[:, 0:width], ACT.Exp, scale=-0.5).then_inc(s.y0, 1)
                    if n == 1:
                        act.activation(s5n[:, 2, :], s5n[:, 1, :], ACT.Exp).then_inc(s.s5_r, 1)

                def ffn(f):
                    k0 = ffn_steps(f)
                    silu(f, 0, 0)
                    hidden_hi(f, 0, 0)
                    round_weights(layer, k0 + 1, 0)
                    silu(f, 1, 1)
                    hidden_hi(f, 1, 1)
                    round_weights(layer, k0 + 1, 1)
                    if f == 0:
                        act.wait_ge(s_params, (layer + 1) * 16)
                        act.activation(s5n[:, 0, :], p_("log_step"), ACT.Exp).then_inc(s.s5_exp, 1)

                    def body(i):
                        silu(f, 2 * i, 0)
                        round_weights(layer, k0 + i, 2)
                        hidden_hi(f, 2 * i, 0, k0 + i, 0)
                        round_weights(layer, k0 + i + 1, 0)
                        silu(f, 2 * i + 1, 1)
                        hidden_hi(f, 2 * i + 1, 1)
                        round_weights(layer, k0 + i + 1, 1)

                    body(1)
                    if f == 0:
                        act.wait_ge(s.s5_red, layer * PER.s5_red + 1)
                        own.link(act.activation(s5n[:, 6, :], s5n[:, 5, :], ACT.Abs))
                        act.activation(s5n[:, 7, :], s5n[:, 5, :], ACT.Sin)
                        act.activation(s5n[:, 8, :], s5n[:, 6, :], ACT.Sin, bias=half_pi_c, scale=-1.0) \
                            .then_inc(s.s5_trig, 1)
                    with act.Fori(2, FT // 2 - 1) as i:
                        body(i)
                    i = FT // 2 - 1
                    silu(f, FT - 2, 0)
                    round_weights(layer, k0 + i, 2)
                    hidden_hi(f, FT - 2, 0, hi=end_hi[f])
                    silu(f, FT - 1, 1)
                    hidden_hi(f, FT - 1, 1, hi=end_hi[f])
                    round_weights(layer, k0 + i + 1, 0)
                    round_weights(layer, k0 + i + 1, 1)
                    for q in range(4):
                        split_pair(layer * PER.u + (4 if f == 0 else 12), q)
                        square_pair(layer * PER.u + (4 if f == 0 else 12), q)

                def last_round(f):
                    round_weights(layer, ffn_steps(f) + FT // 2, 2)

                def softplus_parts(h0):
                    for h in (h0, h0 + 1):
                        act.wait_ge(s.sb_z, layer * PER.sb_z + h + 1)
                        if h >= 2:
                            act.wait_ge(s.sb_sp, layer * PER.sb_sp + h - 1)
                    marks = [own.mark(act.activation(sbt[:, h % 2, :], banks[:, 4 + h % 2, 0:ATT], ACT.Abs))
                             for h in (h0, h0 + 1)]
                    for h in (h0, h0 + 1):
                        own.wait(marks[h % 2])
                        marks[h % 2] = own.mark(act.activation(sbt[:, h % 2, :], sbt[:, h % 2, :], ACT.Exp, scale=-1.0))
                    for h in (h0, h0 + 1):
                        own.wait(marks[h % 2])
                        act.activation(sbt[:, h % 2, :], sbt[:, h % 2, :], ACT.Ln, bias=one_c) \
                            .then_inc(s.sb_ln, 1)

                def branch_hi(n, turn, scale):
                    act.wait_ge(s.y, layer * PER.y + turn + 1)
                    act.activation(b_hi[:, n, :, :], yb[:, turn % 2, :, :], ACT.Copy, scale=scale) \
                        .then_inc(s.b_hi, 1)

                def evacuate(m):
                    bank = banks[:, m % 2, :]
                    name = PROJ[m]
                    act.wait_ge(s.w_used, layer * PER.w_used + FFN_BLOCKS + m + 1 + RING)
                    act.wait_ge(s.rstd, layer * PER.rstd + 2)
                    for tt in range(2):
                        if name in ("dq", "dk"):
                            side = 0 if name == "dq" else 4
                            dst = dqk[:, tt, side:side + 4, :].rearrange("p h d -> p (h d)")
                        else:
                            dst = {"sbv": sbv, "dv": dv, "gv": gv}[name][:, tt, :]
                        ins = act.activation(dst, bank[:, tt * BW:(tt + 1) * BW], ACT.Copy,
                                             scale=rstd_mix[:, T + tt:T + tt + 1])
                    ins.then_inc(s.evac_a, 1)

                def pieces(m):
                    if m in (3, 5):
                        softplus_parts(m - 3)
                    if m in (4, 6):
                        for h in (m - 4, m - 3):
                            act.wait_ge(s.sb_acc, layer * PER.sb_acc + h + 1)
                            act.activation(attA[:, h, :], banks[:, 4 + h % 2, 0:ATT], ACT.Exp) \
                                .then_inc(s.sb_exp, 1)
                    if m == 5:
                        act.wait_ge(s.gla_z, layer * PER.gla_z + 1)
                        own.link(act.activation(gB[:, 0, :], banks[:, 2, 0:T], ACT.Abs, bias=p_("b_gate")))
                        own.link(act.activation(gB[:, 0, :], gB[:, 0, :], ACT.Exp, scale=-1.0))
                        act.activation(gB[:, 0, :], gB[:, 0, :], ACT.Ln, bias=one_c).then_inc(s.gla_ln, 1)
                    if m == 7:
                        act.wait_ge(s.gla_arg, layer * PER.gla_arg + 1)
                        act.activation(kd, kd, ACT.Exp, scale=-1.0 / 16)
                        act.activation(gq[:, :], gq[:, :], ACT.Exp, scale=1.0 / 16).then_inc(s.gla_exp, 1)
                    if m == 8:
                        act.wait_ge(s.gla_kq, layer * PER.gla_kq + 1)
                        act.wait_ge(s.evac_a, layer * PER.evac_a + NTH[SLOT["dk"]])
                        act.activation(ropeX, dqk[:, :, :, :], ACT.Square).then_inc(s.dsa_sq, 1)
                    if m == 9:
                        branch_hi(0, 0, 1.0)
                        act.wait_ge(s.dsa_ms, layer * PER.dsa_ms + 1)
                        own.link(act.activation(dms[:, 2, :], dms[:, 1, :], ACT.Ln))
                        act.activation(dms[:, 2, :], dms[:, 2, :], ACT.Exp, scale=-0.5).then_inc(s.dsa_y0, 1)
                    if m == 12:
                        act.wait_ge(s.dsa_t, layer * PER.dsa_t + 1)
                        act.activation(dqT, banks[:, 6, :], ACT.Copy, scale=0.125).then_inc(s.dsa_qk, 1)
                    if m == 13:
                        act.wait_ge(s.gla_oc, layer * PER.gla_oc + 1)
                        act.activation(gn[:, 1, :], gn[:, 0, :], ACT.Square).then_inc(s.gla_sq, 1)
                        act.wait_ge(s.evac_v, layer * PER.evac_v + NTH[SLOT["gr"]])
                        act.activation(gn[:, 2, :], gr[:, :, :].rearrange("p a t -> p (a t)"), ACT.Tanh, scale=0.5) \
                            .then_inc(s.gla_tanh, 1)
                        act.wait_ge(s.s5_inner, layer * PER.s5_inner + 1)
                        act.activation(s5g[:, 1, :], s5g[:, 1, :], ACT.Tanh).then_inc(s.s5_tanh, 1)
                    if m == 15:
                        act.wait_ge(s.gla_v, layer * PER.gla_v + 1)
                        own.link(act.activation(gn[:, 3, :], gn[:, 1, :], ACT.Ln))
                        act.activation(gn[:, 3, :], gn[:, 3, :], ACT.Exp, scale=-0.5).then_inc(s.gla_y0, 1)
                    if m in (13, 15):
                        for h in (m - 13, m - 12):
                            act.wait_ge(s.dsa_max, layer * PER.dsa_max + h + 1)
                            act.activation(attB[:, h, 0:P], attB[:, h, 0:P], ACT.Exp, bias=dmx[:, h, 0:1])
                            act.activation(attB[:, h, P:ATT], attB[:, h, P:ATT], ACT.Exp, bias=dmx[:, h, 1:2]) \
                                .then_inc(s.dsa_exp, 1)
                    if m in (15, 17):
                        for h in (m - 15, m - 14):
                            act.wait_ge(s.dsa_pt, layer * PER.dsa_pt + h + 1)
                            act.activation(attB[:, h, :], banks[:, 6 + h % 2, 0:ATT], ACT.Copy) \
                                .then_inc(s.dsa_pte, 1)
                    if m == 16:
                        act.wait_ge(s.s5_glu, layer * PER.s5_glu + 1)
                        act.activation(s5g[:, 1, :], banks[:, 5, :], ACT.Tanh, scale=0.25).then_inc(s.s5_sig, 1)
                    if m == 17:
                        branch_hi(2, 1, 0.5)
                    if m == 18:
                        branch_hi(1, 2, 0.25)
                    if m == 20:
                        branch_hi(3, 3, 1.0)

                def mixer():
                    k0 = FFN_BLOCKS // RING
                    for m in range(NPROJ + NGATE):
                        if BY_ACT[m]:
                            evacuate(m)
                        round_weights(layer, k0 + m // RING + 1, m % RING)
                        if m >= NPROJ:
                            g = m - NPROJ
                            act.wait_ge(s.evac_v, layer * PER.evac_v + NTH[m])
                            x = G[:, g // 4, (2 * g) % KT:(2 * g) % KT + 2, :]
                            act.activation(x, x, ACT.Tanh).then_inc(s.tanh, 1)
                        pieces(m)
                    for m in range(NPROJ + NGATE, MIX_BLOCKS - 1):
                        q = m - NPROJ - NGATE
                        for half in range(2):
                            round_half(layer, k0 + m // RING + 1, m % RING, half)
                            if q < NBRANCH:
                                dt = 2 * q + half
                                act.wait_ge(s.mixed, layer * PER.mixed + dt + 1)
                                act.activation(u_hi[:, dt, :], U[:, dt, :], ACT.Copy, scale=0.5) \
                                    .then_inc(s.m_hi, 1)
                        if NBRANCH <= q < NBRANCH + 3:
                            split_pair(layer * PER.u + 8, q - NBRANCH, where=1)
                            square_pair(layer * PER.u + 8, q - NBRANCH)
                    split_pair(layer * PER.u + 8, 3, where=1)
                    square_pair(layer * PER.u + 8, 3)

                norm(0)
                ffn(0)
                last_round(0)
                norm(1)
                mixer()
                round_weights(layer, (FFN_BLOCKS + MIX_BLOCKS) // RING, 2)
                norm(2)
                ffn(1)
                last_round(1)
                assert own.n == PER.act, own.n

        @block.vector
        def _(dve):
            dve.sem_inc(s.w_lo, 2 * RING)

            def half_rest(layer, k, slot, half):
                a = half * HALF
                dve.wait_ge(s.w_hi, layer * PER.w_hi + 2 * (k * RING + slot) + half + 1)
                dve.tensor_tensor(w_lo[:, slot, a:a + HALF], raw[:, slot, a:a + HALF],
                                  w_hi[:, slot, a:a + HALF].bitcast(F32), ALU.subtract).then_inc(s.w_lo, 1)

            def rest_of_weights(layer, k, slot):
                half_rest(layer, k, slot, 0)
                half_rest(layer, k, slot, 1)

            def gain_pair(name, q):
                for kt in (2 * q, 2 * q + 1):
                    ins = dve.tensor_scalar(U[:, kt, :], hT[:, kt, :], p_(name)[:, kt:kt + 1], None, ALU.mult)
                ins.then_inc(s.u, 1)

            def add_squares(done):
                for q in range(4):
                    dve.wait_ge(s.sq, 4 * done + q + 1)
                ins = dve.tensor_tensor(squares[0], squares[0], squares[1], ALU.add)
                ins.then_inc(s.sq_add, 1)
                dve.tensor_tensor(squares[2], squares[2], squares[3], ALU.add).then_inc(s.sq_add, 1)
                dve.wait_ge(s.sq_add, 2 * done + 2)
                dve.tensor_tensor(squares[0], squares[0], squares[2], ALU.add).then_inc(s.sq_sum, 1)

            dve.wait_ge(s_gain, 16)
            for q in range(4):
                if q % 2 == 0:
                    dve.wait_ge(s_x[q // 2], 16)
                gain_pair("g_ffn1", q)
            rest_of_weights(0, 0, 0)
            add_squares(0)
            rest_of_weights(0, 0, 1)
            rest_of_weights(0, 0, 2)
            dve.wait_ge(s_const, 16)
            with dve.Fori(0, LAYERS) as layer:
                own = Steps(dve, s.dve, layer, PER.dve)

                def newton(v, y, t, o):
                    own.link(dve.tensor_tensor(t, y, y, ALU.mult))
                    own.link(dve.tensor_tensor(t, t, v, ALU.mult))
                    own.link(dve.tensor_scalar(t, t, -0.5, 1.5, ALU.mult, ALU.add))
                    own.link(dve.tensor_tensor(o, y, t, ALU.mult))

                def norm(n):
                    w = T + 2 if n == 1 else T
                    v, y, t = n_v[:, 0:w], n_y[:, 0:w], n_t[:, 0:w]
                    dve.wait_ge(s.ss, layer * PER.ss + n + 1)
                    dve.tensor_scalar(v, banks[:, 7, 0:w], -1.0 / D, EPS, ALU.mult, ALU.add).then_inc(s.v, 1)
                    dve.wait_ge(s.y0, layer * PER.y0 + n + 1)
                    own.link(dve.tensor_tensor(t, y, y, ALU.mult))
                    own.link(dve.tensor_tensor(t, t, v, ALU.mult))
                    own.link(dve.tensor_scalar(t, t, -0.5, 1.5, ALU.mult, ALU.add))
                    dve.tensor_tensor((rstd_mix if n == 1 else rstd_ffn)[:, 0:w], y, t, ALU.mult).then_inc(s.rstd, 1)
                    dve.wait_ge(s.rstd, layer * PER.rstd + n + 1)

                def reduce_angles():
                    N = lambda i: s5n[:, i, :]
                    dve.wait_ge(s.s5_exp, layer * PER.s5_exp + 1)
                    dve.tensor_tensor(N(1), p_("lam_re"), N(0), ALU.mult)
                    own.link(dve.tensor_tensor(N(3), p_("lam_im"), N(0), ALU.mult))
                    own.link(dve.tensor_scalar(N(4), N(3), 1.0 / TWO_PI, ROUND, ALU.mult, ALU.add))
                    own.link(dve.tensor_scalar(N(4), N(4), -ROUND, None, ALU.add))
                    at = 3
                    for part in (PI_A, PI_B, PI_C):
                        own.link(dve.scalar_tensor_tensor(out=N(5), in0=N(4), scalar=-part, in1=N(at),
                                                          op0=ALU.mult, op1=ALU.add))
                        at = 5
                    dve.tensor_scalar(N(5), N(5), PI_BELOW, -PI_BELOW, ALU.min, ALU.max).then_inc(s.s5_red, 1)
                    own.mark(dve.tensor_tensor(N(9), p_("lam_re"), p_("lam_re"), ALU.mult))
                    own.link(dve.tensor_tensor(N(10), p_("lam_im"), p_("lam_im"), ALU.mult))
                    own.link(dve.tensor_tensor(N(9), N(9), N(10), ALU.add))
                    dve.reciprocal(N(10), N(9)).then_inc(s.s5_rden, 1)

                def scale(f, j, buf, k, slot, bank=None):
                    dve.wait_ge(s.w_used, layer * PER.w_used + RING * (k) + slot + 1 + RING)
                    if not (isinstance(j, int) and j < 2):
                        dve.wait_ge(s.h_prod, layer * PER.h_prod + FT * f + j - 1)
                    bank = 4 + buf if bank is None else bank
                    dve.tensor_tensor(ab[:, buf, :, :], banks[:, bank, :].rearrange("p (c t) -> p c t", c=2),
                                      rstd_ffn.unsqueeze(1).to_broadcast([P, 2, T]), ALU.mult).then_inc(s.h_ab, 1)

                def product(f, j, buf):
                    dve.wait_ge(s.h_silu, layer * PER.h_silu + FT * f + j + 1)
                    dve.tensor_tensor(hf[:, buf, :], ab[:, buf, 1, :], ab[:, buf, 0, :], ALU.mult) \
                        .then_inc(s.h_prod, 1)

                def hidden_lo(f, j, buf, hi=h_hi, lo=h_lo):
                    dve.wait_ge(s.h_hi, layer * PER.h_hi + FT * f + j + 1)
                    dve.tensor_tensor(lo[:, buf, :], hf[:, buf, :], hi[:, buf, :].bitcast(F32), ALU.subtract) \
                        .then_inc(s.h_lo, 1)

                def ffn(f):
                    k0 = ffn_steps(f)
                    scale(f, 0, 0, k0, 0)
                    product(f, 0, 0)
                    hidden_lo(f, 0, 0)
                    rest_of_weights(layer, k0 + 1, 0)
                    scale(f, 1, 1, k0, 1)
                    product(f, 1, 1)
                    hidden_lo(f, 1, 1)
                    rest_of_weights(layer, k0 + 1, 1)
                    if f == 0:
                        dve.wait_ge(s_params, (layer + 1) * 16)
                        reduce_angles()

                    def body(i, bank=4):
                        scale(f, 2 * i, 0, k0 + i - 1, 2, bank)
                        product(f, 2 * i, 0)
                        rest_of_weights(layer, k0 + i, 2)
                        hidden_lo(f, 2 * i, 0)
                        rest_of_weights(layer, k0 + i + 1, 0)
                        scale(f, 2 * i + 1, 1, k0 + i, 1)
                        product(f, 2 * i + 1, 1)
                        hidden_lo(f, 2 * i + 1, 1)
                        rest_of_weights(layer, k0 + i + 1, 1)

                    body(1, bank=6)
                    with dve.Fori(2, FT // 2 - 1) as i:
                        body(i)
                    i = FT // 2 - 1
                    scale(f, FT - 2, 0, k0 + i - 1, 2)
                    product(f, FT - 2, 0)
                    rest_of_weights(layer, k0 + i, 2)
                    hidden_lo(f, FT - 2, 0, end_hi[f], end_lo[f])
                    scale(f, FT - 1, 1, k0 + i, 0)
                    product(f, FT - 1, 1)
                    hidden_lo(f, FT - 1, 1, end_hi[f], end_lo[f])
                    rest_of_weights(layer, k0 + i + 1, 0)
                    if f == 1:
                        dve.wait_ge(s_params, (layer + 2) * 16)
                    for q in range(4):
                        if q < 3:
                            dve.wait_ge(s.ffn_acc, layer * PER.ffn_acc + 3 * f + q + 1)
                        else:
                            dve.wait_ge(s.w_used, layer * PER.w_used + RING * (k0 + FT // 2 - 1) + 2 + 1 + RING)
                        dve.scalar_tensor_tensor(out=hT[:, 2 * q:2 * q + 2, :].rearrange("p a t -> p (a t)"),
                                                 in0=banks[:, q, :], scalar=0.5,
                                                 in1=hT[:, 2 * q:2 * q + 2, :].rearrange("p a t -> p (a t)"),
                                                 op0=ALU.mult, op1=ALU.add).then_inc(s.res, 1)
                        dve.wait_ge(s.res, layer * PER.res + 8 * f + q + 1)
                        gain_pair("g_mix" if f == 0 else "g_ffn1", q)
                    rest_of_weights(layer, k0 + i + 1, 1)
                    add_squares(layer * 3 + (1 if f == 0 else 3))

                def last_rest(f):
                    rest_of_weights(layer, ffn_steps(f) + FT // 2, 2)

                def s5_rotate(i):
                    dve.wait_ge(s.s5_p, layer * PER.s5_p + i + 1)
                    if i == 0:
                        dve.wait_ge(s.s5_tab, layer * PER.s5_tab + 1)
                    if i >= 2:
                        dve.wait_ge(s.s5_state, layer * PER.s5_state + i - 1)
                    bank = banks[:, 6 + i % 2, :].rearrange("p (c t) -> p c t", c=2)
                    x = s5x[:, i % 2, :, :, :]
                    dve.tensor_tensor(x[:, 0, 0, :], bank[:, 0, :], rotC[:, i, :], ALU.mult)
                    dve.tensor_tensor(x[:, 0, 1, :], bank[:, 1, :], rotC[:, i, :], ALU.mult)
                    dve.tensor_tensor(x[:, 1, 0, :], bank[:, 1, :], rotS[:, i, :], ALU.mult)
                    dve.tensor_tensor(x[:, 1, 1, :], bank[:, 0, :], rotS[:, i, :], ALU.mult).then_inc(s.s5_rot, 1)

                def s5_scan(i):
                    dve.wait_ge(s.s5_x, layer * PER.s5_x + i + 1)
                    decay = s5n[:, 2, i:i + 1].to_broadcast([P, T])
                    for part in range(2):
                        ins = dve.tensor_tensor_scan(s5x[:, i % 2, 1, part, :], decay, s5x[:, i % 2, 0, part, :],
                                                     0.0, ALU.mult, ALU.add)
                    ins.then_inc(s.s5_scan, 1)

                def branch_lo(n, turn, scale):
                    dve.wait_ge(s.b_hi, layer * PER.b_hi + turn + 1)
                    dve.scalar_tensor_tensor(out=b_lo[:, n, :, :], in0=yb[:, turn % 2, :, :], scalar=scale,
                                             in1=b_hi[:, n, :, :].bitcast(F32), op0=ALU.mult, op1=ALU.subtract) \
                        .then_inc(s.b_lo, 1)

                def dilated_softmax(h):
                    dve.wait_ge(s.dsa_s, layer * PER.dsa_s + h + 1)
                    own.mark(dve.tensor_tensor(attB[:, h, 0:P], banks[:, 6 + h % 2, 0:P], c("forbid")[:, P:T], ALU.add))
                    own.link(dve.tensor_tensor(attB[:, h, P:ATT], banks[:, 6 + h % 2, P:ATT], c("forbid"), ALU.add))
                    dve.tensor_reduce(dmx[:, h, 0:1], attB[:, h, 0:P], AX.X, ALU.max, negate=True)
                    dve.tensor_reduce(dmx[:, h, 1:2], attB[:, h, P:ATT], AX.X, ALU.max, negate=True) \
                        .then_inc(s.dsa_max, 1)

                def dilated_weights(h):
                    dve.wait_ge(s.dsa_exp, layer * PER.dsa_exp + h + 1)
                    count = c("count")
                    dve.tensor_tensor_reduce(attB[:, h, 0:P], attB[:, h, 0:P], count[:, P:T], 1.0, 0.0,
                                             ALU.mult, ALU.add, dmx[:, h, 2:3])
                    own.link(dve.tensor_tensor_reduce(attB[:, h, P:ATT], attB[:, h, P:ATT], count, 1.0, 0.0,
                                                      ALU.mult, ALU.add, dmx[:, h, 3:4]))
                    own.link(dve.reciprocal(dmx[:, h, 4:6], dmx[:, h, 2:4]))
                    dve.tensor_scalar(attB[:, h, 0:P], attB[:, h, 0:P], dmx[:, h, 4:5], None, ALU.mult)
                    dve.tensor_scalar(attB[:, h, P:ATT], attB[:, h, P:ATT], dmx[:, h, 5:6], None, ALU.mult) \
                        .then_inc(s.dsa_p, 1)

                def gla_mask(h):
                    dve.wait_ge(s.gla_att, layer * PER.gla_att + h + 1)
                    dve.scalar_tensor_tensor(out=attA[:, h, :], in0=banks[:, 4 + h % 2, 0:ATT], scalar=3e38,
                                             in1=c("causal"), op0=ALU.min, op1=ALU.mult).then_inc(s.gla_attm, 1)

                def pieces(m):
                    if 1 <= m <= ST:
                        s5_scan(m - 1)
                    if m in (3, 5):
                        for h in (m - 3, m - 2):
                            dve.wait_ge(s.sb_ln, layer * PER.sb_ln + h + 1)
                            own.link(dve.scalar_tensor_tensor(out=attA[:, h, :], in0=banks[:, 4 + h % 2, 0:ATT],
                                                              scalar=0.0, in1=sbt[:, h % 2, :], op0=ALU.max,
                                                              op1=ALU.add))
                            dve.tensor_tensor(attA[:, h, :], attA[:, h, :], c("strict"), ALU.mult) \
                                .then_inc(s.sb_sp, 1)
                    if m in (4, 6):
                        for h in (m - 4, m - 3):
                            dve.wait_ge(s.sb_exp, layer * PER.sb_exp + h + 1)
                            dve.scalar_tensor_tensor(out=attA[:, h, :], in0=attA[:, h, :], scalar=3e38,
                                                     in1=c("strict"), op0=ALU.min, op1=ALU.mult) \
                                .then_inc(s.sb_w, 1)
                    if m == 5:
                        dve.wait_ge(s.gla_ln, layer * PER.gla_ln + 1)
                        dve.tensor_scalar(gB[:, 1, :], banks[:, 2, 0:T], p_("b_gate"), 0.0, ALU.add, ALU.min) \
                            .then_inc(s.gla_zread, 1)
                        dve.wait_ge(s.gla_zread, layer * PER.gla_zread + 1)
                        own.link(dve.tensor_tensor(gB[:, 1, :], gB[:, 1, :], gB[:, 0, :], ALU.subtract))
                        own.link(dve.tensor_tensor_scan(gB[:, 2, :], one_c.to_broadcast([P, T]), gB[:, 1, :], 0.0,
                                                        ALU.mult, ALU.add))
                    if m == 7:
                        for i in range(NGC):
                            at, n = (P * i, P) if i < 4 else (P * 4 + T * (i - 4), T)
                            mid = gB[:, 2, GC * i + GC // 2 - 1:GC * i + GC // 2]
                            dve.tensor_scalar(kd[:, at:at + n], gB[:, 2, 0:n], mid, -GLA_CLIP, ALU.subtract, ALU.max)
                            ins = dve.tensor_scalar(gq[:, GC * i:GC * i + GC], gB[:, 2, GC * i:GC * i + GC], mid,
                                                    GLA_CLIP, ALU.subtract, ALU.min)
                        ins.then_inc(s.gla_arg, 1)
                        dve.wait_ge(s.gla_exp, layer * PER.gla_exp + 1)
                        near = kd[:, 0:4 * P].rearrange("p (i t) -> p i t", i=4)
                        far = kd[:, 4 * P:6 * T].rearrange("p (i t) -> p i t", i=4)
                        dve.tensor_tensor(near, near, gqk[:, 1, 0:P].unsqueeze(1).to_broadcast([P, 4, P]), ALU.mult)
                        dve.tensor_tensor(far, far, gqk[:, 1, :].unsqueeze(1).to_broadcast([P, 4, T]), ALU.mult)
                        dve.scalar_tensor_tensor(out=gq[:, :], in0=gq[:, :], scalar=float(32 ** -0.5),
                                                 in1=gqk[:, 0, :], op0=ALU.mult, op1=ALU.mult) \
                            .then_inc(s.gla_kq, 1)
                    if m == 8:
                        dve.wait_ge(s.sb_o, layer * PER.sb_o + 1)
                        dve.tensor_copy(yb[:, 0, :, :].rearrange("p a t -> p (a t)"), banks[:, 2, :]) \
                            .then_inc(s.y, 1)
                    if m == 9:
                        gla_mask(0), gla_mask(1)
                        dve.wait_ge(s.dsa_sq, layer * PER.dsa_sq + 1)
                        own.link(dve.tensor_reduce(dms[:, 0, :], ropeX.rearrange("p t h d -> p (t h) d"),
                                                   AX.X, ALU.add))
                        dve.tensor_scalar(dms[:, 1, :], dms[:, 0, :], 1.0 / 64, EPS, ALU.mult, ALU.add) \
                            .then_inc(s.dsa_ms, 1)
                    if m == 10:
                        gla_mask(2), gla_mask(3)
                        branch_lo(0, 0, 1.0)
                        dve.wait_ge(s.dsa_y0, layer * PER.dsa_y0 + 1)
                        newton(dms[:, 1, :], dms[:, 2, :], dms[:, 3, :], dms[:, 4, :])
                        flat = dqk[:, :, :, :].rearrange("p t h d -> p (t h) d")
                        own.link(dve.tensor_tensor(flat, flat, dms[:, 4, :].unsqueeze(2).to_broadcast([P, 16, 64]),
                                                   ALU.mult))
                        a = PARAM["dsa_gain"][0]
                        for side in range(2):
                            gain = prm[:, a + 64 * side:a + 64 * side + 64]
                            x = dqk[:, :, 4 * side:4 * side + 4, :]
                            n = own.mark(dve.tensor_tensor(
                                x, x, gain.unsqueeze(1).unsqueeze(1).to_broadcast([P, 2, 4, 64]), ALU.mult))
                        own.wait(n)
                    if m == 11:
                        for tt in range(2):
                            x = dqk[:, tt, :, :]
                            sin = c("sin")[:, 64 * tt:64 * tt + 64].unsqueeze(1).to_broadcast([P, 8, 64])
                            dve.tensor_tensor(ropeX[:, tt, :, 0:32], x[:, :, 32:64], sin[:, :, 0:32], ALU.mult)
                            n = own.mark(dve.tensor_tensor(ropeX[:, tt, :, 32:64], x[:, :, 0:32], sin[:, :, 32:64],
                                                           ALU.mult))
                        own.wait(n)
                        for tt in range(2):
                            x = dqk[:, tt, :, :]
                            cos = c("cos")[:, 64 * tt:64 * tt + 64].unsqueeze(1).to_broadcast([P, 8, 64])
                            n = own.mark(dve.tensor_tensor(x, x, cos, ALU.mult))
                        own.wait(n)
                        dve.tensor_tensor(dqk[:, :, :, :], dqk[:, :, :, :], ropeX, ALU.add).then_inc(s.dsa_rope, 1)
                    if m == 12:
                        dve.wait_ge(s.gla_o, layer * PER.gla_o + 1)
                        dve.tensor_copy(gn[:, 0, :], banks[:, 2, :]).then_inc(s.gla_oc, 1)
                        dve.wait_ge(s.dsa_t, layer * PER.dsa_t + 1)
                        dve.tensor_copy(dkT, banks[:, 7, :]).then_inc(s.dsa_qk, 1)
                        dve.wait_ge(s.s5_y, layer * PER.s5_y + ST)
                        for k in range(2):
                            n = own.mark(dve.scalar_tensor_tensor(
                                out=s5g[:, 0, k * T:(k + 1) * T], in0=s5u[:, k, :], scalar=p_("s5_d")[:, k:k + 1],
                                in1=banks[:, 3, k * T:(k + 1) * T], op0=ALU.mult, op1=ALU.add))
                        own.wait(n)
                        own.link(dve.tensor_tensor(s5g[:, 1, :], s5g[:, 0, :], s5g[:, 0, :], ALU.mult))
                        root = math.sqrt(2 / math.pi)
                        own.link(dve.tensor_scalar(s5g[:, 1, :], s5g[:, 1, :], 0.044715 * root, root,
                                                   ALU.mult, ALU.add))
                        dve.tensor_tensor(s5g[:, 1, :], s5g[:, 1, :], s5g[:, 0, :], ALU.mult) \
                            .then_inc(s.s5_inner, 1)
                    if m == 13:
                        dilated_softmax(0), dilated_softmax(1)
                    if m == 14:
                        dve.wait_ge(s.gla_ss, layer * PER.gla_ss + 1)
                        dve.tensor_scalar(gn[:, 1, :], banks[:, 4, :], 1.0 / 64, EPS, ALU.mult, ALU.add) \
                            .then_inc(s.gla_v, 1)
                        dve.wait_ge(s.s5_tanh, layer * PER.s5_tanh + 1)
                        dve.scalar_tensor_tensor(out=s5g[:, 2, :], in0=s5g[:, 1, :], scalar=1.0, in1=s5g[:, 0, :],
                                                 op0=ALU.add, op1=ALU.mult).then_inc(s.s5_gelu, 1)
                        dilated_weights(0), dilated_weights(1)
                        dilated_softmax(2), dilated_softmax(3)
                    if m == 15:
                        dve.wait_ge(s.gla_tanh, layer * PER.gla_tanh + 1)
                        own.link(dve.scalar_tensor_tensor(out=gn[:, 2, :], in0=gn[:, 2, :], scalar=1.0,
                                                          in1=gr[:, :, :].rearrange("p a t -> p (a t)"),
                                                          op0=ALU.add, op1=ALU.mult))
                    if m == 16:
                        dilated_weights(2), dilated_weights(3)
                        dve.wait_ge(s.gla_y0, layer * PER.gla_y0 + 1)
                        t = yb[:, 1, :, :].rearrange("p a t -> p (a t)")
                        newton(gn[:, 1, :], gn[:, 3, :], t, gn[:, 3, :])
                        own.link(dve.tensor_tensor(gn[:, 0, :], gn[:, 0, :], gn[:, 3, :], ALU.mult))
                        for k in range(2):
                            ins = dve.scalar_tensor_tensor(
                                out=yb[:, 1, k, :], in0=gn[:, 0, k * T:(k + 1) * T], scalar=p_("gla_norm")[:, k:k + 1],
                                in1=gn[:, 2, k * T:(k + 1) * T], op0=ALU.mult, op1=ALU.mult)
                        ins.then_inc(s.y, 1)
                    if m == 17:
                        dve.wait_ge(s.b_lo, layer * PER.b_lo + 1)
                        dve.wait_ge(s.s5_sig, layer * PER.s5_sig + 1)
                        dve.scalar_tensor_tensor(out=yb[:, 0, :, :].rearrange("p a t -> p (a t)"),
                                                 in0=s5g[:, 1, :], scalar=1.0, in1=banks[:, 4, :],
                                                 op0=ALU.add, op1=ALU.mult).then_inc(s.y, 1)
                    if m == 18:
                        branch_lo(2, 1, 0.5)
                    if m == 19:
                        branch_lo(1, 2, 0.25)
                        dve.wait_ge(s.b_lo, layer * PER.b_lo + 2)
                        dve.wait_ge(s.dsa_o, layer * PER.dsa_o + 1)
                        dve.tensor_copy(yb[:, 1, :, :].rearrange("p a t -> p (a t)"), banks[:, 3, :]) \
                            .then_inc(s.y, 1)
                    if m == 21:
                        branch_lo(3, 3, 1.0)

                def gate(dt):
                    q = dt // 2
                    if dt % 2 == 0:
                        dve.wait_ge(s.pb_half, layer * PER.pb_half + q + 1)
                    else:
                        k = NPROJ + NGATE + q
                        dve.wait_ge(s.w_used, layer * PER.w_used + RING * ((FFN_BLOCKS + k) // RING) + (FFN_BLOCKS + k) % RING + 1 + RING)
                    if dt == 0:
                        dve.wait_ge(s.tanh, layer * PER.tanh + NGATE)
                    if dt >= 2:
                        dve.wait_ge(s.mixed, layer * PER.mixed + dt - 1)
                    bank = (4 if q % 2 == 0 else 0) + 2 * (dt % 2)
                    dve.scalar_tensor_tensor(
                        out=prods[dt % 2], in0=G[:, :, dt, :], scalar=1.0,
                        in1=banks[:, bank:bank + 2, :].rearrange("p b (n t) -> p (b n) t", n=2),
                        op0=ALU.add, op1=ALU.mult).then_inc(s.gated, 1)

                def mixed_lo(dt):
                    dve.wait_ge(s.m_hi, layer * PER.m_hi + dt + 1)
                    dve.scalar_tensor_tensor(out=u_lo[:, dt, :], in0=U[:, dt, :], scalar=0.5,
                                             in1=u_hi[:, dt, :].bitcast(F32), op0=ALU.mult, op1=ALU.subtract) \
                        .then_inc(s.m_lo, 1)

                def evacuate(m):
                    dve.wait_ge(s.w_used, layer * PER.w_used + FFN_BLOCKS + m + 1 + RING)
                    bank, factor = banks[:, m % 2, :].rearrange("p (c t) -> p c t", c=2), 1.0
                    if m >= NPROJ:
                        g = m - NPROJ
                        if g == NGATE // 2:
                            dve.wait_ge(s.s5_state, layer * PER.s5_state + ST)
                        dst, factor = G[:, g // 4, (2 * g) % KT:(2 * g) % KT + 2, :], 0.5
                    elif PROJ[m] == "gg":
                        dst, bank = gq[:, :].unsqueeze(1), bank[:, 0:1, :]
                    else:
                        dst = {"s5u": s5u, "sbq": sbq, "sbk": sbk, "gqk": gqk, "gr": gr}[PROJ[m]][:, :, :]
                        factor = 0.125 if PROJ[m] == "sbq" else 1.0
                    n = 1 if m < NPROJ and PROJ[m] == "gg" else 2
                    dve.scalar_tensor_tensor(out=dst, in0=bank, scalar=factor,
                                             in1=rstd_mix[:, 0:T].unsqueeze(1).to_broadcast([P, n, T]),
                                             op0=ALU.mult, op1=ALU.mult).then_inc(s.evac_v, 1)

                def mixer():
                    k0 = FFN_BLOCKS // RING
                    for m in range(NPROJ + NGATE):
                        if not BY_ACT[m]:
                            evacuate(m)
                        if 1 <= m <= ST:
                            s5_rotate(m - 1)
                        rest_of_weights(layer, k0 + m // RING + 1, m % RING)
                        pieces(m)
                    for q in range(NBRANCH):
                        m = NPROJ + NGATE + q
                        gate(2 * q)
                        if q > 0:
                            mixed_lo(2 * q - 2)
                        half_rest(layer, k0 + m // RING + 1, m % RING, 0)
                        gate(2 * q + 1)
                        if q > 0:
                            mixed_lo(2 * q - 1)
                        half_rest(layer, k0 + m // RING + 1, m % RING, 1)
                    mixed_lo(6)
                    mixed_lo(7)
                    for o, tiles in enumerate(OUT_TILES):
                        m = NPROJ + NGATE + NBRANCH + o
                        q = tiles[0] // 2
                        if o != 3:
                            dve.wait_ge(s.w_used, layer * PER.w_used + RING * (k0 + m // RING) + m % RING + 1 + RING)
                            x = hT[:, 2 * q:2 * q + 2, :].rearrange("p a t -> p (a t)")
                            dve.tensor_tensor(x, banks[:, 4 + q, :], x, ALU.add).then_inc(s.res, 1)
                            dve.wait_ge(s.res, layer * PER.res + 4 + q + 1)
                            gain_pair("g_ffn2", q)
                        if o < 4:
                            rest_of_weights(layer, k0 + m // RING + 1, m % RING)

                norm(0)
                ffn(0)
                last_rest(0)
                norm(1)
                mixer()
                add_squares(layer * 3 + 2)
                rest_of_weights(layer, (FFN_BLOCKS + MIX_BLOCKS) // RING, 2)
                norm(2)
                ffn(1)
                last_rest(1)
                assert own.n == PER.dve, own.n

        @block.gpsimd
        def _(pool):
            def split_stream(done, where=0):
                for q in range(4):
                    pool.wait_ge(s.u_hi, done + q + 1)
                    pool.tensor_tensor(in_lo[where][:, 2 * q:2 * q + 2, :], U[:, 2 * q:2 * q + 2, :],
                                       in_hi[where][:, 2 * q:2 * q + 2, :].bitcast(F32), ALU.subtract).then_inc(s.u_lo, 1)

            split_stream(0)
            pool.wait_ge(s_const, 16)
            with pool.Fori(0, LAYERS) as layer:
                own = Steps(pool, s.pool, layer, PER.pool)

                def tt(o, a, b, op):
                    own.link(pool.tensor_tensor(o, a, b, op))

                N = lambda i: s5n[:, i, :]

                def const(i, shape=(P, ST)):
                    return c("scalars")[:, i:i + 1].to_broadcast(list(shape))

                one, zero, minus_half, three_halves = (const(i) for i in (2, 3, 4, 5))

                def unit(cn, sn):
                    tt(N(11), N(cn), N(cn), ALU.mult)
                    tt(N(12), N(sn), N(sn), ALU.mult)
                    tt(N(11), N(11), N(12), ALU.add)
                    tt(N(11), N(11), minus_half, ALU.mult)
                    tt(N(11), N(11), three_halves, ALU.add)
                    tt(N(cn), N(cn), N(11), ALU.mult)
                    tt(N(sn), N(sn), N(11), ALU.mult)

                def rotations():
                    pool.wait_ge(s.s5_trig, layer * PER.s5_trig + 1)
                    tt(rotC[:, :, 0], one, one, ALU.mult)
                    tt(rotS[:, :, 0], one, one, ALU.subtract)
                    tt(N(13), N(8), one, ALU.mult)
                    tt(N(14), N(7), one, ALU.mult)
                    unit(13, 14)
                    w = 1
                    while w < T:
                        ta = tabA[:, 0:ST * w].rearrange("p (i t) -> p i t", i=ST)
                        tb = tabB[:, 0:ST * w].rearrange("p (i t) -> p i t", i=ST)
                        cz = N(13).unsqueeze(2).to_broadcast([P, ST, w])
                        sz = N(14).unsqueeze(2).to_broadcast([P, ST, w])
                        tt(ta, rotC[:, :, 0:w], cz, ALU.mult)
                        tt(tb, rotS[:, :, 0:w], sz, ALU.mult)
                        tt(rotC[:, :, w:2 * w], ta, tb, ALU.subtract)
                        tt(ta, rotC[:, :, 0:w], sz, ALU.mult)
                        tt(tb, rotS[:, :, 0:w], cz, ALU.mult)
                        if 2 * w == T:
                            pool.tensor_tensor(rotS[:, :, w:2 * w], ta, tb, ALU.add).then_inc(s.s5_tab, 1)
                        else:
                            tt(rotS[:, :, w:2 * w], ta, tb, ALU.add)
                        if 2 * w < T:
                            tt(N(15), N(13), N(13), ALU.mult)
                            tt(N(16), N(14), N(14), ALU.mult)
                            tt(N(17), N(13), N(14), ALU.mult)
                            tt(N(13), N(15), N(16), ALU.subtract)
                            tt(N(14), N(17), N(17), ALU.add)
                            unit(13, 14)
                        w *= 2

                def coefficients():
                    pool.wait_ge(s.s5_r, layer * PER.s5_r + 1)
                    pool.wait_ge(s.s5_rden, layer * PER.s5_rden + 1)
                    tt(N(19), N(2), N(8), ALU.mult)
                    tt(N(19), N(19), one, ALU.subtract)
                    tt(N(20), N(2), N(7), ALU.mult)
                    tt(N(11), N(19), p_("lam_re"), ALU.mult)
                    tt(N(12), N(20), p_("lam_im"), ALU.mult)
                    tt(N(21), N(11), N(12), ALU.add)
                    tt(N(21), N(21), N(10), ALU.mult)
                    tt(N(11), N(20), p_("lam_re"), ALU.mult)
                    tt(N(12), N(19), p_("lam_im"), ALU.mult)
                    tt(N(22), N(11), N(12), ALU.subtract)
                    tt(N(22), N(22), N(10), ALU.mult)
                    tt(N(23), zero, N(21), ALU.subtract)
                    tt(N(24), zero, N(22), ALU.subtract)
                    a = PARAM["s5_c"][0]
                    c_re = prm[:, a:a + ST * 32].rearrange("p (i h) -> p i h", i=ST)
                    c_im = prm[:, a + ST * 32:a + 2 * ST * 32].rearrange("p (i h) -> p i h", i=ST)
                    t = tabA[:, 0:ST * 32].rearrange("p (i h) -> p i h", i=ST)
                    wide = lambda i: N(i).unsqueeze(2).to_broadcast([P, ST, 32])
                    tt(t, c_im, wide(24), ALU.mult)
                    tt(s5c[:, 0, :, :], c_re, wide(21), ALU.mult)
                    tt(s5c[:, 0, :, :], s5c[:, 0, :, :], t, ALU.add)
                    tt(t, c_im, wide(23), ALU.mult)
                    tt(s5c[:, 1, :, :], c_re, wide(24), ALU.mult)
                    pool.tensor_tensor(s5c[:, 1, :, :], s5c[:, 1, :, :], t, ALU.add).then_inc(s.s5_coef, 1)

                def s5_tile(i):
                    x = s5x[:, i % 2, :, :, :]
                    pool.wait_ge(s.s5_rot, layer * PER.s5_rot + i + 1)
                    n = own.mark(pool.tensor_tensor(x[:, 0, 0, :], x[:, 0, 0, :], x[:, 1, 0, :], ALU.add))
                    pool.tensor_tensor(x[:, 0, 1, :], x[:, 0, 1, :], x[:, 1, 1, :], ALU.subtract) \
                        .then_inc(s.s5_x, 1)
                    own.wait(n)
                    pool.wait_ge(s.s5_scan, layer * PER.s5_scan + i + 1)
                    if i >= 2:
                        pool.wait_ge(s.s5_y, layer * PER.s5_y + i - 1)
                    own.mark(pool.tensor_tensor(x[:, 0, 0, :], x[:, 1, 0, :], rotC[:, i, :], ALU.mult))
                    own.mark(pool.tensor_tensor(x[:, 0, 1, :], x[:, 1, 1, :], rotC[:, i, :], ALU.mult))
                    re, im = st[:, i % 2, 0, :], st[:, i % 2, 1, :]
                    own.mark(pool.tensor_tensor(re, x[:, 1, 1, :], rotS[:, i, :], ALU.mult))
                    own.link(pool.tensor_tensor(im, x[:, 1, 0, :], rotS[:, i, :], ALU.mult))
                    tt(re, x[:, 0, 0, :], re, ALU.subtract)
                    pool.tensor_tensor(im, x[:, 0, 1, :], im, ALU.add).then_inc(s.s5_state, 1)

                def mix(dt):
                    pool.wait_ge(s.gated, layer * PER.gated + dt + 1)
                    p = prods[dt % 2]
                    tt(p[:, 0:2, :], p[:, 0:2, :], p[:, 2:4, :], ALU.add)
                    pool.tensor_tensor(U[:, dt, :], p[:, 0, :], p[:, 1, :], ALU.add).then_inc(s.mixed, 1)

                pool.wait_ge(s_params, (layer + 1) * 16)
                rotations()
                split_stream(layer * PER.u_hi + 4)
                coefficients()
                for i in range(ST):
                    s5_tile(i)
                for dt in range(KT):
                    mix(dt)
                split_stream(layer * PER.u_hi + 8, where=1)
                split_stream(layer * PER.u_hi + 12)
                assert own.n == PER.pool, own.n

    return nc


def _constants():
    k = np.zeros((P, NCONST), np.float32)

    def put(name, a):
        at, n = CONST[name]
        k[:, at:at + n] = np.asarray(a, np.float32).reshape(P, n)

    r = np.arange(P)
    put("ident", np.eye(P))
    put("head_ones", (r[:, None] // 64 == r[None, :] // 64))
    put("neg_suffix", -(r[:, None] >= r[None, :]).astype(np.float32))
    put("neg_ones", -np.ones((P, P)))
    key = np.concatenate([np.tile(r[:, None], (1, T)), np.tile(r[:, None] + P, (1, P))], 1)
    query = np.concatenate([np.tile(np.arange(T), (P, 1)), np.tile(np.arange(P, T), (P, 1))], 1)
    put("causal", key <= query)
    put("strict", key < query)
    gap = r[:, None] + P - np.arange(T)[None, :]
    count = np.zeros((P, T), np.float32)
    for window, dil in ((128, 1), (512, 4), (2048, 16)):
        count += (gap >= 0) & (gap % dil == 0) & (gap // dil <= window // dil)
    put("count", count)
    put("forbid", np.where(count > 0, 0.0, -1e30))
    inv = np.float32(10000.0) ** (-np.arange(0, 64, 2, dtype=np.float32) / np.float32(64))
    ang = (np.arange(T, dtype=np.float32)[:, None] * inv[None, :].astype(np.float32)).astype(np.float64)
    cos, sin = np.cos(ang), np.sin(ang)
    both = lambda a, b: np.concatenate([a, b], 1).reshape(2, P, 64).transpose(1, 0, 2)
    put("cos", both(cos, cos))
    put("sin", both(-sin, sin))
    put("scalars", np.tile(np.array([EPS, math.pi / 2, 1.0, 0.0, -0.5, 1.5]), (P, 1)))
    return k


def _rows(w):
    return w.reshape(w.shape[0] // P, P, w.shape[1]).transpose(1, 0, 2)


def _stream(ffn1_w_in, ffn1_w_out, w_in, w_branch, w_out, ffn2_w_in, ffn2_w_out):
    s = np.zeros((LAYERS * PER_LAYER + RING, P, BLK), np.float32)

    def ffn(at, w_i, w_o):
        a = _rows(w_i).reshape(P, KT, 2, FT, P).transpose(3, 0, 1, 2, 4).reshape(FT, P, BLK)
        o = w_o.reshape(FT // 2, 2, P, D).transpose(0, 2, 1, 3).reshape(FT // 2, P, BLK)
        s[at], s[at + 1] = a[0], a[1]
        for i in range(1, FT // 2 - 1):
            s[at + 3 * i - 1], s[at + 3 * i], s[at + 3 * i + 1] = a[2 * i], o[i - 1], a[2 * i + 1]
        s[at + FFN_BLOCKS - 4:at + FFN_BLOCKS] = a[-2], a[-1], o[-2], o[-1]

    first = {"sbq": 0, "sbk": 256, "sbv": 512, "s5u": 768, "gqk": 1024, "gv": 1280, "gr": 1536, "gg": 1792,
             "dq": 1808, "dk": 2064, "dv": 2320}
    gates = 2576
    for layer in range(LAYERS):
        at = layer * PER_LAYER
        ffn(at, ffn1_w_in[layer], ffn1_w_out[layer])
        at += FFN_BLOCKS
        rows = _rows(w_in[layer])
        for name in PROJ:
            if name == "gg":
                s[at].reshape(P, KT, 256)[:, :, 0:16] = rows[:, :, 1792:1808]
            else:
                s[at] = rows[:, :, first[name]:first[name] + 256].reshape(P, BLK)
            at += 1
        for g in range(NGATE):
            s[at] = rows[:, :, gates + 256 * g:gates + 256 * (g + 1)].reshape(P, BLK)
            at += 1
        rows = w_branch[layer].reshape(4, 2, P, D).transpose(2, 0, 1, 3).reshape(P, 8, D)
        for q in range(NBRANCH):
            s[at] = rows[:, :, 256 * q:256 * (q + 1)].reshape(P, BLK)
            at += 1
        rows = _rows(w_out[layer])
        for tiles in OUT_TILES:
            n = len(tiles) * P
            s[at][:, 0:KT * n] = rows[:, :, tiles[0] * P:tiles[0] * P + n].reshape(P, KT * n)
            at += 1
        ffn(at, ffn2_w_in[layer], ffn2_w_out[layer])
    return s


def _params(i):
    k = np.zeros((LAYERS + 1, P, NPARAM), np.float32)
    for layer in range(LAYERS):
        def put(name, a):
            at, n = PARAM[name]
            k[layer, 0:a.shape[0], at:at + n] = a.reshape(a.shape[0], n)

        tiles = lambda a: a.reshape(-1, P).T
        put("g_ffn1", tiles(i["ffn1_norm"][layer]))
        put("g_mix", tiles(i["mix_norm"][layer]))
        put("g_ffn2", tiles(i["ffn2_norm"][layer]))
        put("gla_norm", tiles(i["gla_norm"][layer]))
        put("b_gate", tiles(i["gla_b_gate"][layer]))
        put("s5_d", tiles(i["s5_d"][layer].reshape(-1)))
        put("lam_re", tiles(i["s5_lam_re"][layer].reshape(-1)))
        put("lam_im", tiles(i["s5_lam_im"][layer].reshape(-1)))
        put("log_step", tiles(np.repeat(i["s5_log_step"][layer], 64)))
        put("dsa_gain", np.broadcast_to(np.concatenate([i["dsa_q_norm"][layer], i["dsa_k_norm"][layer]]), (P, 128)))
        put("w_gate", i["gla_w_gate"][layer])
        b = np.zeros((2, 2, P, P), np.float32)
        c = np.zeros((2, P, ST, 32), np.float32)
        for part, (bm, cm) in enumerate([("s5_b_re", "s5_c_re"), ("s5_b_im", "s5_c_im")]):
            for g in range(16):
                t, e = g // 2, g % 2
                b[part, t // 4, 32 * (t % 4) + 16 * e:32 * (t % 4) + 16 * e + 16, 64 * e:64 * e + 64] = \
                    i[bm][layer][g].T
                c[part, 64 * e:64 * e + 64, t, 16 * e:16 * e + 16] = i[cm][layer][g].T
        put("s5_b", b.transpose(2, 0, 1, 3))
        put("s5_c", c.transpose(1, 0, 2, 3))
        put("w_glu", _rows(i["s5_w_glu"][layer]))
    return k


def kernel(**inputs):
    import concourse.bacc as _bacc
    from concourse.bass_utils import run_bass_kernel_spmd as _run

    i = {name: np.asarray(a) for name, a in inputs.items()}
    arrays = {
        "x_t": np.ascontiguousarray(_rows(i["x"][0].T)),
        "weights": _stream(i["ffn1_w_in"], i["ffn1_w_out"], i["w_in"], i["w_branch"], i["w_out"],
                           i["ffn2_w_in"], i["ffn2_w_out"]),
        "params": _params(i),
        "constants": _constants(),
    }
    nc = _bacc.Bacc("TRN2", target_bir_lowering=False, num_devices=1, dynamic_dma_scratch_size=1024)
    args = [nc.dram_tensor(n, a.shape, F32, kind="ExternalInput").ap() for n, a in arrays.items()]
    args.append(nc.dram_tensor("out_t", (P, KT, T), F32, kind="ExternalOutput").ap())
    build(nc, *args)
    r = _run(nc, [arrays], core_ids=[0])
    return r.results[0]["out_t"].transpose(1, 0, 2).reshape(D, T).T.reshape(1, T, D)
```
